# Optimizing a Trainium2 kernel written in Bass

```python
import jax, jax.numpy as jnp
from jax import lax
import numpy as np

D_MODEL = 1024
BATCH = 1
SEQ = 256
DEPTH = 2

N_EVEN = (DEPTH + 1) // 2
N_ODD = DEPTH // 2
NORM_EPS = 1e-6
D_FF = 2816

CONV_WIDTH = D_MODEL // 2
CONV_GROUPS = 8
CONV_TAPS = 3
RWKV_WIDTH = D_MODEL - CONV_WIDTH
RWKV_HEAD = 64
RWKV_HEADS = RWKV_WIDTH // RWKV_HEAD
DECAY_RANK = 32
ICLR_RANK = 32
GATE_RANK = 96
RWKV_GN_EPS = 64e-5
RWKV_SHIFT_COLS = 3 * RWKV_WIDTH + DECAY_RANK + ICLR_RANK + GATE_RANK
EVEN_IN = 3 * CONV_WIDTH + RWKV_SHIFT_COLS
_RWKV_SPLITS = (RWKV_WIDTH, 2 * RWKV_WIDTH, 3 * RWKV_WIDTH,
                3 * RWKV_WIDTH + DECAY_RANK, 3 * RWKV_WIDTH + DECAY_RANK + ICLR_RANK)

MLA_HEADS = 8
Q_RANK = 384
KV_RANK = 256
NOPE_DIM = 128
ROPE_DIM = 64
V_DIM = 128
QK_DIM = NOPE_DIM + ROPE_DIM
ODD_IN = Q_RANK + KV_RANK + ROPE_DIM
ROPE_THETA = 10000.0
Q_BLOCK = 128
ATTN_SCALE = QK_DIM ** -0.5


def _rmsnorm(x, gain, eps=NORM_EPS):
    xf = x.astype(jnp.float32)
    y = xf * lax.rsqrt(jnp.mean(xf * xf, axis=-1, keepdims=True) + eps)
    return (y * gain.astype(jnp.float32)).astype(x.dtype)

def _swiglu(h, w_gate, w_up, w_down):
    return (jax.nn.silu(h @ w_gate) * (h @ w_up)) @ w_down

def _shift(u):
    return jnp.pad(u, ((0, 0), (1, 0), (0, 0)))[:, :-1]

def _short_conv(u, w):
    T = u.shape[1]
    up = jnp.pad(u, ((0, 0), (CONV_TAPS - 1, 0), (0, 0)))
    return sum(up[:, j:j + T] * w[j] for j in range(CONV_TAPS))

def _rwkv7_scan(r, decay, k, v, a_vec, b_vec):
    B, T, H, N = r.shape

    def step(S, inp):
        r_t, w_t, k_t, v_t, a_t, b_t = inp
        Sa = jnp.einsum('bhvk,bhk->bhv', S, a_t)
        S = S * w_t[:, :, None, :] + Sa[..., None] * b_t[:, :, None, :] + v_t[..., None] * k_t[:, :, None, :]
        return S, jnp.einsum('bhvk,bhk->bhv', S, r_t)

    xs = tuple(jnp.moveaxis(t, 1, 0) for t in (r, decay, k, v, a_vec, b_vec))
    S0 = jnp.zeros((B, H, N, N), jnp.float32)
    _, y = lax.scan(step, S0, xs)
    return jnp.moveaxis(y, 0, 1)

def _conv_rwkv_mixer(h, w_in, conv_w, mu_shift, w0, w_up, a0, a_up, g_up,
                     k_k, k_a, r_k, ln_w, ln_b, w_out):
    B, T, _ = h.shape
    f32 = jnp.float32
    p = h @ w_in
    p_conv, p_rwkv = p[..., :3 * CONV_WIDTH], p[..., 3 * CONV_WIDTH:]
    gate_b, gate_c, h_in = jnp.split(p_conv, 3, axis=-1)
    y_conv = gate_b * _short_conv(gate_c * h_in, conv_w)
    p_rwkv = p_rwkv + (_shift(p_rwkv) - p_rwkv) * mu_shift
    r, k, v, dw, da, dg = jnp.split(p_rwkv, _RWKV_SPLITS, axis=-1)
    log_w = -jax.nn.softplus(-(w0 + jnp.tanh(dw) @ w_up).astype(f32)) - 0.5
    decay = jnp.exp(-jnp.exp(log_w))
    a = jax.nn.sigmoid((a0 + da @ a_up).astype(f32))
    g = jax.nn.sigmoid(dg) @ g_up

    def heads(t):
        return t.astype(f32).reshape(B, T, RWKV_HEADS, RWKV_HEAD)

    r_h, v_h, a_h, decay_h = heads(r), heads(v), heads(a), heads(decay)
    kk = heads(k * k_k)
    kk = kk * lax.rsqrt(jnp.maximum(jnp.sum(kk * kk, axis=-1, keepdims=True), 1e-24))
    k_h = heads(k) * (1.0 + (a_h - 1.0) * k_a.astype(f32).reshape(RWKV_HEADS, RWKV_HEAD))
    y = _rwkv7_scan(r_h, decay_h, k_h, v_h, -kk, kk * a_h)
    mu = jnp.mean(y, axis=-1, keepdims=True)
    var = jnp.mean(jnp.square(y - mu), axis=-1, keepdims=True)
    y = (y - mu) * lax.rsqrt(var + RWKV_GN_EPS) * ln_w.astype(f32).reshape(RWKV_HEADS, RWKV_HEAD) \
        + ln_b.astype(f32).reshape(RWKV_HEADS, RWKV_HEAD)
    y = y + jnp.sum(r_h * k_h * r_k.astype(f32), axis=-1, keepdims=True) * v_h
    y_rwkv = y.reshape(B, T, RWKV_WIDTH).astype(h.dtype) * g
    return jnp.concatenate([y_conv, y_rwkv], axis=-1) @ w_out

def _rope(t, cos, sin):
    t1, t2 = t[..., :ROPE_DIM // 2], t[..., ROPE_DIM // 2:]
    return jnp.concatenate([t1 * cos - t2 * sin, t2 * cos + t1 * sin], axis=-1)

def _causal_attention(q, k, v):
    B, T, H, Dk = q.shape
    nb = T // Q_BLOCK
    qb = q.reshape(B, nb, Q_BLOCK, H, Dk).transpose(1, 0, 3, 2, 4)
    kpos = jnp.arange(T)

    def one_block(args):
        qi, i = args
        s = jnp.einsum('bhqd,bkhd->bhqk', qi, k, preferred_element_type=jnp.float32) * ATTN_SCALE
        qpos = i * Q_BLOCK + jnp.arange(Q_BLOCK)
        s = jnp.where(kpos[None, :] <= qpos[:, None], s, jnp.finfo(jnp.float32).min)
        p = jax.nn.softmax(s, axis=-1)
        return jnp.einsum('bhqk,bkhd->bqhd', p.astype(v.dtype), v)

    out = lax.map(one_block, (qb, jnp.arange(nb)))
    return out.transpose(1, 0, 2, 3, 4).reshape(B, T, H, v.shape[-1])

def _mla_mixer(h, cos, sin, w_in, q_a_norm, kv_a_norm, w_q_up, w_kv_up, q_norm, k_norm, w_out):
    B, T, _ = h.shape
    p = h @ w_in
    c_q, c_kv, k_pe = jnp.split(p, (Q_RANK, Q_RANK + KV_RANK), axis=-1)
    q = (_rmsnorm(c_q, q_a_norm) @ w_q_up).reshape(B, T, MLA_HEADS, QK_DIM)
    kv = (_rmsnorm(c_kv, kv_a_norm) @ w_kv_up).reshape(B, T, MLA_HEADS, NOPE_DIM + V_DIM)
    k_nope, v = kv[..., :NOPE_DIM], kv[..., NOPE_DIM:]
    k = jnp.concatenate([k_nope, jnp.broadcast_to(k_pe[:, :, None, :], (B, T, MLA_HEADS, ROPE_DIM))], axis=-1)
    q = _rmsnorm(q, q_norm)
    k = _rmsnorm(k, k_norm)
    q = jnp.concatenate([q[..., :NOPE_DIM], _rope(q[..., NOPE_DIM:], cos, sin)], axis=-1)
    k = jnp.concatenate([k[..., :NOPE_DIM], _rope(k[..., NOPE_DIM:], cos, sin)], axis=-1)
    o = _causal_attention(q, k, v)
    return o.reshape(B, T, MLA_HEADS * V_DIM) @ w_out

def first_inputs(seed: int = 0) -> dict:
    key = jax.random.key(seed)
    ks = iter(jax.random.split(key, 32))
    f32 = jnp.float32

    def nrm(shape, fan_in):
        return jax.random.normal(next(ks), shape, f32) * fan_in ** -0.5

    def gain(shape):
        return 1.0 + 0.02 * jax.random.normal(next(ks), shape, f32)

    def unif(shape, lo, hi):
        return jax.random.uniform(next(ks), shape, f32, lo, hi)

    x = jax.random.normal(next(ks), (BATCH, SEQ, D_MODEL), f32)
    offset = jax.random.randint(next(ks), (BATCH, 1), 0, 1024, jnp.int32)
    positions = (offset + jnp.arange(SEQ, dtype=jnp.int32)[None, :]).astype(jnp.int32)
    return {
        "x": x,
        "positions": positions,
        "norm_gains": gain((DEPTH, 3, D_MODEL)),
        "ffn_w_gate": nrm((DEPTH, 2, D_MODEL, D_FF), D_MODEL),
        "ffn_w_up": nrm((DEPTH, 2, D_MODEL, D_FF), D_MODEL),
        "ffn_w_down": nrm((DEPTH, 2, D_FF, D_MODEL), D_FF),
        "even_w_in": nrm((N_EVEN, D_MODEL, EVEN_IN), D_MODEL),
        "even_conv_w": nrm((N_EVEN, CONV_TAPS, CONV_WIDTH), CONV_TAPS),
        "even_mu_shift": unif((N_EVEN, RWKV_SHIFT_COLS), 0.0, 1.0),
        "rwkv_w0": unif((N_EVEN, RWKV_WIDTH), -6.0, 0.0),
        "rwkv_w_up": nrm((N_EVEN, DECAY_RANK, RWKV_WIDTH), DECAY_RANK),
        "rwkv_a0": 0.1 * jax.random.normal(next(ks), (N_EVEN, RWKV_WIDTH), f32),
        "rwkv_a_up": nrm((N_EVEN, ICLR_RANK, RWKV_WIDTH), ICLR_RANK),
        "rwkv_g_up": nrm((N_EVEN, GATE_RANK, RWKV_WIDTH), GATE_RANK),
        "rwkv_k_k": 0.85 + 0.05 * jax.random.normal(next(ks), (N_EVEN, RWKV_WIDTH), f32),
        "rwkv_k_a": gain((N_EVEN, RWKV_WIDTH)),
        "rwkv_r_k": 0.1 * jax.random.normal(next(ks), (N_EVEN, RWKV_HEADS, RWKV_HEAD), f32),
        "rwkv_ln_w": gain((N_EVEN, RWKV_WIDTH)),
        "rwkv_ln_b": 0.02 * jax.random.normal(next(ks), (N_EVEN, RWKV_WIDTH), f32),
        "even_w_out": nrm((N_EVEN, CONV_WIDTH + RWKV_WIDTH, D_MODEL), CONV_WIDTH + RWKV_WIDTH),
        "odd_w_in": nrm((N_ODD, D_MODEL, ODD_IN), D_MODEL),
        "mla_q_a_norm": gain((N_ODD, Q_RANK)),
        "mla_kv_a_norm": gain((N_ODD, KV_RANK)),
        "mla_w_q_up": nrm((N_ODD, Q_RANK, MLA_HEADS * QK_DIM), Q_RANK),
        "mla_w_kv_up": nrm((N_ODD, KV_RANK, MLA_HEADS * (NOPE_DIM + V_DIM)), KV_RANK),
        "mla_q_norm": gain((N_ODD, QK_DIM)),
        "mla_k_norm": gain((N_ODD, QK_DIM)),
        "odd_w_out": nrm((N_ODD, MLA_HEADS * V_DIM, D_MODEL), MLA_HEADS * V_DIM),
    }

def first_block(x, positions, norm_gains, ffn_w_gate, ffn_w_up, ffn_w_down,
              even_w_in, even_conv_w, even_mu_shift, rwkv_w0, rwkv_w_up, rwkv_a0, rwkv_a_up,
              rwkv_g_up, rwkv_k_k, rwkv_k_a, rwkv_r_k, rwkv_ln_w, rwkv_ln_b, even_w_out,
              odd_w_in, mla_q_a_norm, mla_kv_a_norm, mla_w_q_up, mla_w_kv_up,
              mla_q_norm, mla_k_norm, odd_w_out):
    inv_freq = ROPE_THETA ** (-jnp.arange(0, ROPE_DIM, 2, dtype=jnp.float32) / ROPE_DIM)
    ang = positions.astype(jnp.float32)[..., None] * inv_freq
    cos = jnp.cos(ang)[:, :, None, :].astype(x.dtype)
    sin = jnp.sin(ang)[:, :, None, :].astype(x.dtype)

    for layer in range(DEPTH):
        g = norm_gains[layer]
        x = x + 0.5 * _swiglu(_rmsnorm(x, g[0]), ffn_w_gate[layer, 0], ffn_w_up[layer, 0], ffn_w_down[layer, 0])
        h = _rmsnorm(x, g[1])
        if layer % 2 == 0:
            i = layer // 2
            mix = _conv_rwkv_mixer(h, even_w_in[i], even_conv_w[i], even_mu_shift[i], rwkv_w0[i],
                                   rwkv_w_up[i], rwkv_a0[i], rwkv_a_up[i], rwkv_g_up[i], rwkv_k_k[i],
                                   rwkv_k_a[i], rwkv_r_k[i], rwkv_ln_w[i], rwkv_ln_b[i], even_w_out[i])
        else:
            j = layer // 2
            mix = _mla_mixer(h, cos, sin, odd_w_in[j], mla_q_a_norm[j], mla_kv_a_norm[j], mla_w_q_up[j],
                             mla_w_kv_up[j], mla_q_norm[j], mla_k_norm[j], odd_w_out[j])
        x = x + mix.astype(x.dtype)
        x = x + 0.5 * _swiglu(_rmsnorm(x, g[2]), ffn_w_gate[layer, 1], ffn_w_up[layer, 1], ffn_w_down[layer, 1])
    return x


DEPTH_2 = 1

CHUNK = 64
D_CONV = 512
CONV_WIDTH_2 = 31
N_HEADS = 8
HEAD_DIM = 64
D_ATTN = N_HEADS * HEAD_DIM
D_MIX = D_CONV + D_ATTN
EPS = 1e-6
N_IN = 2 * D_CONV + 3 * D_ATTN + N_HEADS


def rms_norm(x, g):
    xf = x.astype(jnp.float32)
    y = xf * lax.rsqrt(jnp.mean(xf * xf, axis=-1, keepdims=True) + EPS)
    return (y * g.astype(jnp.float32)).astype(x.dtype)

def layer_norm(x, g, b):
    xf = x.astype(jnp.float32)
    mu = jnp.mean(xf, axis=-1, keepdims=True)
    xc = xf - mu
    y = xc * lax.rsqrt(jnp.mean(xc * xc, axis=-1, keepdims=True) + EPS)
    return (y * g.astype(jnp.float32) + b.astype(jnp.float32)).astype(x.dtype)

def swiglu_ffn(h, w13, w2):
    gate, up = jnp.split(h @ w13, 2, axis=-1)
    return (jax.nn.silu(gate) * up) @ w2

def conv_module(a, g, conv_w, conv_b, ln_g, ln_b):
    u = a * jax.nn.sigmoid(g)
    u_pad = jnp.pad(u, ((0, 0), (CONV_WIDTH_2 - 1, 0), (0, 0)))
    y = lax.conv_general_dilated(
        u_pad, conv_w[:, None, :].astype(u.dtype), window_strides=(1,), padding="VALID",
        dimension_numbers=("NWC", "WIO", "NWC"), feature_group_count=D_CONV)
    y = y + conv_b.astype(y.dtype)
    y = layer_norm(y, ln_g, ln_b)
    return jax.nn.silu(y)

def forgetting_attention(q, k, v, f_logit):
    seq = q.shape[1]
    log_f = jax.nn.log_sigmoid(f_logit.astype(jnp.float32))
    cum = jnp.cumsum(log_f, axis=1).transpose(0, 2, 1)
    scale = HEAD_DIM ** -0.5
    outs = []
    for i in range(seq // Q_BLOCK):
        q0, q1 = i * Q_BLOCK, (i + 1) * Q_BLOCK
        qb, kb, vb = q[:, q0:q1], k[:, :q1], v[:, :q1]
        s = jnp.einsum("bqhd,bkhd->bhqk", qb, kb, preferred_element_type=jnp.float32) * scale
        s = s + cum[:, :, q0:q1, None] - cum[:, :, None, :q1]
        qpos = jnp.arange(q0, q1)
        kpos = jnp.arange(q1)
        s = jnp.where(kpos[None, :] <= qpos[:, None], s, -jnp.inf)
        p = jax.nn.softmax(s, axis=-1)
        outs.append(jnp.einsum("bhqk,bkhd->bqhd", p.astype(vb.dtype), vb))
    return jnp.concatenate(outs, axis=1)

def second_inputs(seed: int = 0) -> dict:
    key = jax.random.key(seed)
    ks = jax.random.split(key, 24)
    f32 = jnp.float32

    def nrm(k, shape, scale):
        return jax.random.normal(k, shape, f32) * scale

    def gain(k, shape):
        return 1.0 + 0.05 * jax.random.normal(k, shape, f32)

    L = DEPTH_2
    return {
        "x": jax.random.normal(ks[0], (BATCH, SEQ, D_MODEL), f32),
        "ffn1_norm": gain(ks[1], (L, D_MODEL)),
        "ffn1_w13": nrm(ks[2], (L, D_MODEL, 2 * D_FF), D_MODEL ** -0.5),
        "ffn1_w2": nrm(ks[3], (L, D_FF, D_MODEL), D_FF ** -0.5),
        "mix_norm": gain(ks[4], (L, D_MODEL)),
        "w_in": nrm(ks[5], (L, D_MODEL, N_IN), D_MODEL ** -0.5),
        "conv_w": nrm(ks[6], (L, CONV_WIDTH_2, D_CONV), CONV_WIDTH_2 ** -0.5),
        "conv_b": nrm(ks[7], (L, D_CONV), 0.02),
        "conv_ln_g": gain(ks[8], (L, D_CONV)),
        "conv_ln_b": nrm(ks[9], (L, D_CONV), 0.02),
        "forget_b": jax.random.uniform(ks[10], (L, N_HEADS), f32, minval=1.0, maxval=4.0),
        "out_norm_conv": gain(ks[11], (L, D_CONV)),
        "out_norm_attn": gain(ks[12], (L, D_ATTN)),
        "w_out": nrm(ks[13], (L, D_MIX, D_MODEL), D_MIX ** -0.5),
        "ffn2_norm": gain(ks[14], (L, D_MODEL)),
        "ffn2_w13": nrm(ks[15], (L, D_MODEL, 2 * D_FF), D_MODEL ** -0.5),
        "ffn2_w2": nrm(ks[16], (L, D_FF, D_MODEL), D_FF ** -0.5),
        "final_norm": gain(ks[17], (D_MODEL,)),
    }

def second_block(x, ffn1_norm, ffn1_w13, ffn1_w2, mix_norm, w_in, conv_w, conv_b, conv_ln_g,
              conv_ln_b, forget_b, out_norm_conv, out_norm_attn, w_out, ffn2_norm, ffn2_w13,
              ffn2_w2, final_norm):
    bsz, seq, _ = x.shape
    splits = [D_CONV, 2 * D_CONV, 2 * D_CONV + D_ATTN, 2 * D_CONV + 2 * D_ATTN,
              2 * D_CONV + 3 * D_ATTN]
    for l in range(DEPTH_2):
        x = x + 0.5 * swiglu_ffn(rms_norm(x, ffn1_norm[l]), ffn1_w13[l], ffn1_w2[l])

        h = rms_norm(x, mix_norm[l])
        proj = h @ w_in[l]
        a, g, q, k, v, fl = jnp.split(proj, splits, axis=-1)

        y_conv = conv_module(a, g, conv_w[l], conv_b[l], conv_ln_g[l], conv_ln_b[l])

        heads = (bsz, seq, N_HEADS, HEAD_DIM)
        y_attn = forgetting_attention(q.reshape(heads), k.reshape(heads), v.reshape(heads),
                                      fl + forget_b[l].astype(fl.dtype))
        y_attn = y_attn.reshape(bsz, seq, D_ATTN)

        y = jnp.concatenate([rms_norm(y_conv, out_norm_conv[l]),
                             rms_norm(y_attn, out_norm_attn[l])], axis=-1)
        x = x + y @ w_out[l]

        x = x + 0.5 * swiglu_ffn(rms_norm(x, ffn2_norm[l]), ffn2_w13[l], ffn2_w2[l])
    return rms_norm(x, final_norm)


def setup_inputs(seed=0):
    out = dict(first_inputs(seed))
    for name, value in second_inputs(seed + 1).items():
        if name != "x":
            out[name + "_2"] = value
    return out


def reference(
    x, positions, norm_gains, ffn_w_gate, ffn_w_up, ffn_w_down, even_w_in, even_conv_w,
    even_mu_shift, rwkv_w0, rwkv_w_up, rwkv_a0, rwkv_a_up, rwkv_g_up, rwkv_k_k, rwkv_k_a,
    rwkv_r_k, rwkv_ln_w, rwkv_ln_b, even_w_out, odd_w_in, mla_q_a_norm, mla_kv_a_norm,
    mla_w_q_up, mla_w_kv_up, mla_q_norm, mla_k_norm, odd_w_out, ffn1_norm_2, ffn1_w13_2,
    ffn1_w2_2, mix_norm_2, w_in_2, conv_w_2, conv_b_2, conv_ln_g_2, conv_ln_b_2, forget_b_2,
    out_norm_conv_2, out_norm_attn_2, w_out_2, ffn2_norm_2, ffn2_w13_2, ffn2_w2_2, final_norm_2,
):
    x = first_block(
        x, positions, norm_gains, ffn_w_gate, ffn_w_up, ffn_w_down, even_w_in, even_conv_w,
        even_mu_shift, rwkv_w0, rwkv_w_up, rwkv_a0, rwkv_a_up, rwkv_g_up, rwkv_k_k, rwkv_k_a,
        rwkv_r_k, rwkv_ln_w, rwkv_ln_b, even_w_out, odd_w_in, mla_q_a_norm, mla_kv_a_norm,
        mla_w_q_up, mla_w_kv_up, mla_q_norm, mla_k_norm, odd_w_out,
    )
    return second_block(
        x, ffn1_norm_2, ffn1_w13_2, ffn1_w2_2, mix_norm_2, w_in_2, conv_w_2, conv_b_2,
        conv_ln_g_2, conv_ln_b_2, forget_b_2, out_norm_conv_2, out_norm_attn_2, w_out_2,
        ffn2_norm_2, ffn2_w13_2, ffn2_w2_2, final_norm_2,
    )


_drawn_inputs = setup_inputs


def setup_inputs(seed=0):
    import zlib

    import numpy as np

    out = dict(_drawn_inputs(seed))
    spreads = {}
    factors = {'rwkv_w_up': 3.009,
     'rwkv_k_k': 4.663,
     'rwkv_k_a': 7.826,
     'rwkv_ln_w': 8.0,
     'rwkv_ln_b': 5.745,
     'mla_q_a_norm': 8.0,
     'mla_kv_a_norm': 8.0,
     'mla_q_norm': 8.0,
     'mla_k_norm': 8.0,
     'ffn1_norm_2': 3.399,
     'conv_b_2': 3.432,
     'conv_ln_b_2': 7.648,
     'out_norm_conv_2': 12.328,
     'ffn2_norm_2': 4.72,
     'mix_norm_2': 3.93,
     'conv_ln_g_2': 4.027,
     'out_norm_attn_2': 8.0}
    for name, (base, spread) in spreads.items():
        noise = np.random.default_rng([zlib.crc32(name.encode()), seed]).standard_normal(out[name].shape)
        drawn = base * np.exp(spread * noise) if base else spread * noise
        out[name] = __import__('jax').numpy.asarray(drawn.astype(out[name].dtype))
    for name, factor in factors.items():
        out[name] = (out[name] * factor).astype(out[name].dtype)
    return out
```

```python
from contextlib import ExitStack

import numpy as np

import concourse.bass as bass
from concourse import mybir

F32 = mybir.dt.float32
F32R = mybir.dt.float32r
I32 = mybir.dt.int32
ALU = mybir.AluOpType
ACT = mybir.ActivationFunctionType
X = mybir.AxisListType.X

P = 128
T = 256
D = 1024
KD = D // P
F_FF = 2816
NORM_EPS = 1e-6
GU, DN = 2048, 1024
FFN_UNITS = F_FF // P
UNITS = {"ffn": FFN_UNITS, "even": 12, "mla": 8, "fox": 10}
STAGES = ("ffn", "even", "ffn", "ffn", "mla", "ffn", "ffn", "fox", "ffn")
NORMS = len(STAGES)

RW = 512
HEADS = 8
DECAY_RANK, ICLR_RANK, GATE_RANK = 32, 32, 96
CONV_TAPS = 3
CHUNK = 64
LOG_W = float(np.exp(-0.5))
GN_EPS = 64e-5
KK_SHIFT = 17
Q_RANK, KV_RANK, NOPE, ROPE, V_DIM = 384, 256, 128, 64, 128
QK_DIM = NOPE + ROPE
MLA_SCALE = QK_DIM ** -0.5
FOX_DIM = 64
FOX_SCALE = FOX_DIM ** -0.5
LONG_TAPS = 31
PAD = LONG_TAPS - 1
MASKED = -3.0e38
TWO_PI = (6.28125, 0.0019350051879882812, 2.0 * np.pi - 6.28125 - 0.0019350051879882812)


class Steps:

    def __init__(self, sem, names):
        self.sem, self.value, self.finished = sem, {n: i + 1 for i, n in enumerate(names)}, 0
        assert len(self.value) == len(names)

    def done(self, instruction, name):
        self.finished += 1
        assert self.value[name] == self.finished, (name, self.value[name], self.finished)
        instruction.then_inc(self.sem, 1)


LEVELS = (2, 4, 8, 16, 32)
CONST_COLS = {}
_at = 0
for _name, _n in (("ident", P), ("ones", P), ("head_ones", P), ("rot", ROPE), ("inv_freq", 1),
                  ("before", P), ("not_after", P), ("pairs", P), *((f"join{n}", P) for n in LEVELS),
                  ("causal", 3 * P)):
    CONST_COLS[_name] = slice(_at, _at + _n)
    _at += _n
CONSTS = _at


def shape_constants():
    out = np.zeros((P, CONSTS), np.float32)
    s, t = np.arange(P)[:, None], np.arange(P)[None, :]
    put = lambda name, value: out[:value.shape[0], CONST_COLS[name]].__setitem__(Ellipsis, value)
    put("ident", (s == t) * 1.0)
    put("head_ones", (s // 64 == t // 64) * 1.0)
    put("ones", np.ones((P, P)))
    half = ROPE // 2
    i, o = np.arange(ROPE)[:, None], np.arange(ROPE)[None, :]
    put("rot", (i == o - half) * 1.0 - (i == o + half) * 1.0)
    freq = np.float32(10000.0) ** (-np.arange(0, ROPE, 2, dtype=np.float32) / np.float32(ROPE))
    put("inv_freq", np.concatenate([freq, freq])[:, None])
    same = s // CHUNK == t // CHUNK
    put("before", (same & (s < t)) * 1.0)
    put("not_after", (same & (s <= t)) * 1.0)
    put("pairs", ((s // 2 == t // 2) & (s < t)) * 1.0)
    for n in LEVELS:
        put(f"join{n}", ((s // (2 * n) == t // (2 * n)) & (s // n < t // n)) * 1.0)
    diagonal = np.where(t <= s, 0.0, MASKED)
    put("causal", np.concatenate([diagonal, np.zeros((P, P)), diagonal], 1))
    return out


PARAM_COLS = {}
_at = 0
for _name, _n in (("norms", NORMS * KD), ("conv_w", CONV_TAPS * 4), ("mu", 14), ("w0", 4), ("a0", 4),
                  ("k_k", 4), ("k_a", 4), ("r_k", 4), ("ln_w", 4), ("ln_b", 4), ("q_a", 3), ("kv_a", 2),
                  ("q_nope", 1), ("q_rope", 1), ("k_nope", 1), ("k_rope", 1), ("long_w", LONG_TAPS * 4),
                  ("long_b", 4), ("cln_g", 4), ("cln_b", 4), ("out_conv", 4), ("out_attn", 4), ("forget_b", 1)):
    PARAM_COLS[_name] = slice(_at, _at + _n)
    _at += _n
PARAMS = _at


def columns(v):
    v = np.asarray(v).reshape(-1, v.shape[-1])
    return v.reshape(v.shape[0], -1, P).transpose(2, 0, 1).reshape(P, -1)


def parameter_columns(a):
    out = np.zeros((P, PARAMS), np.float32)

    def put(name, value, row=0):
        out[row:row + value.shape[0], PARAM_COLS[name]][:, :value.shape[1]] = value

    ng = np.asarray(a["norm_gains"])
    put("norms", columns(np.concatenate([ng.reshape(6, D), np.asarray(a["ffn1_norm_2"]),
                                         np.asarray(a["mix_norm_2"]), np.asarray(a["ffn2_norm_2"])])))
    put("conv_w", columns(a["even_conv_w"][0]))
    mu = np.asarray(a["even_mu_shift"])[0]
    put("mu", columns(mu[:3 * RW]))
    low = DECAY_RANK + ICLR_RANK
    out[:low, PARAM_COLS["mu"].start + 12] = mu[3 * RW:3 * RW + low]
    out[:GATE_RANK, PARAM_COLS["mu"].start + 13] = mu[3 * RW + low:]
    for name, key in (("w0", "rwkv_w0"), ("a0", "rwkv_a0"), ("k_k", "rwkv_k_k"), ("k_a", "rwkv_k_a"),
                      ("ln_w", "rwkv_ln_w"), ("ln_b", "rwkv_ln_b"), ("q_a", "mla_q_a_norm"),
                      ("kv_a", "mla_kv_a_norm"), ("long_b", "conv_b_2"), ("cln_g", "conv_ln_g_2"),
                      ("cln_b", "conv_ln_b_2"), ("out_conv", "out_norm_conv_2"), ("out_attn", "out_norm_attn_2")):
        put(name, columns(a[key]))
    put("r_k", columns(np.asarray(a["rwkv_r_k"]).reshape(1, RW)))
    put("long_w", columns(a["conv_w_2"][0]))
    for name, key in (("q", "mla_q_norm"), ("k", "mla_k_norm")):
        v = np.asarray(a[key])[0][:, None]
        put(name + "_nope", v[:NOPE])
        put(name + "_rope", v[NOPE:])
    for row in (0, 64):
        put("forget_b", np.asarray(a["forget_b_2"])[0][:, None], row)
    return out


def blocks(w, cols=P):
    w = np.asarray(w)
    k, n = w.shape
    return w.reshape(k // P, P, n // cols, cols).transpose(2, 1, 0, 3).reshape(n // cols, P, -1)


def rows(w):
    return np.asarray(w).reshape(-1, P, w.shape[-1])


def weight_units(a):
    units = []

    def add(gu, dn=()):
        u = np.zeros((P, GU + DN), np.float32)
        for base, parts in ((0, gu), (GU, dn)):
            for part in parts:
                u[:, base:base + part.shape[1]] = part
                base += part.shape[1]
        units.append(u)

    def threes(parts):
        for i in range(0, len(parts), 3):
            add(parts[i:i + 2], parts[i + 2:i + 3])

    def ffn(gate, up, down):
        for g, u, d in zip(blocks(gate), blocks(up), rows(down)):
            add([g, u], [d])

    fg, fu, fd = (np.asarray(a[f"ffn_w_{n}"]) for n in ("gate", "up", "down"))
    ffn(fg[0, 0], fu[0, 0], fd[0, 0])
    w = np.asarray(a["even_w_in"])[0]
    conv, rkv, low = w[:, :3 * RW], w[:, 3 * RW:6 * RW], w[:, 6 * RW:]
    threes(list(blocks(rkv)))
    add([blocks(low[:, :64], 64)[0], blocks(low[:, 64:], GATE_RANK)[0]])
    threes(list(blocks(conv)))
    threes(list(rows(a["even_w_out"][0])))
    ffn(fg[0, 1], fu[0, 1], fd[0, 1])
    ffn(fg[1, 0], fu[1, 0], fd[1, 0])
    w = np.asarray(a["odd_w_in"])[0]
    b = list(blocks(w[:, :Q_RANK + KV_RANK]))
    add(b[0:2], b[2:3])
    add(b[3:5], [blocks(w[:, Q_RANK + KV_RANK:], ROPE)[0]])
    w = np.asarray(a["mla_w_q_up"])[0].reshape(Q_RANK, HEADS, QK_DIM)
    u = blocks(w[:, :, :NOPE].reshape(Q_RANK, -1)).transpose(1, 0, 2).reshape(P, -1)
    add([u[:, :GU]], [u[:, GU:]])
    rope = blocks(w[:, :, NOPE:].reshape(Q_RANK, -1), ROPE).transpose(1, 0, 2).reshape(P, -1)
    w = np.asarray(a["mla_w_kv_up"])[0].reshape(KV_RANK, HEADS, NOPE + V_DIM)
    v = rows(w[:, :, NOPE:].reshape(KV_RANK, -1))
    add(list(blocks(w[:, :, :NOPE].reshape(KV_RANK, -1))), [v[0]])
    add([v[1], rope[:, :GU - D]], [rope[:, GU - D:]])
    threes(list(rows(a["odd_w_out"][0])))
    ffn(fg[1, 1], fu[1, 1], fd[1, 1])

    def ffn2(w13, w2):
        w13 = np.asarray(w13)[0]
        ffn(w13[:, :F_FF], w13[:, F_FF:], w2[0])

    ffn2(a["ffn1_w13_2"], a["ffn1_w2_2"])
    w = np.asarray(a["w_in_2"])[0]
    b = list(blocks(w[:, :4 * RW]))
    threes(b[:15])
    v = list(rows(w[:, 4 * RW:5 * RW]))
    add([b[15], v[0], v[1]], v[2:4])
    fl = np.zeros((D, 72), np.float32)
    fl[:, :8] = fl[:, 64:] = w[:, 5 * RW:]
    add(v[4:], [blocks(fl, 72)[0]])
    w = list(rows(a["w_out_2"][0]))
    threes(w[4:] + w[:4])
    ffn2(a["ffn2_w13_2"], a["ffn2_w2_2"])
    units = np.stack(units)
    return np.ascontiguousarray(units[:, :, :GU]), np.ascontiguousarray(units[:, :, GU:])


def build(nc, units_gu, units_dn, x_in, positions, constants, params, low_rank, final_gain, out, stages=STAGES):
    first_pair, n_units = [], 0
    for kind in stages:
        first_pair.append(n_units // 2)
        n_units += UNITS[kind]
    last_unit = [2 * b + UNITS[k] for b, k in zip(first_pair, stages)]

    with ExitStack() as ctx:
        def sb(name, shape, dt=F32):
            return ctx.enter_context(nc.sbuf_tensor(name, shape, dt))

        def sem(name):
            return ctx.enter_context(nc.semaphore(name))

        raw_gu = sb("raw_gu", [P, 2, GU])
        raw_dn = sb("raw_dn", [P, 2, DN])
        gu_hi, gu_lo = sb("gu_hi", [P, 2, GU], F32R), sb("gu_lo", [P, 2, GU], F32R)
        dn_hi, dn_lo = sb("dn_hi", [P, 2, DN], F32R), sb("dn_lo", [P, 2, DN], F32R)
        x = sb("x", [P, 2, D])
        h_hi, h_lo = sb("h_hi", [P, KD, T], F32R), sb("h_lo", [P, KD, T], F32R)
        silu = sb("silu", [P, 2, T])
        act32 = sb("act32", [P, 2, T])
        act_hi, act_lo = sb("act_hi", [P, 2, T], F32R), sb("act_lo", [P, 2, T], F32R)
        warm = sb("warm", [P, 1])
        sumsq, rstd, rstd_half = sb("sumsq", [P, 2]), sb("rstd", [P, 2]), sb("rstd_half", [P, 2])
        eps_col = sb("eps_col", [P, 3])
        cst = sb("cst", [P, CONSTS])
        par = sb("par", [P, PARAMS])
        lora = sb("lora", [P, 2, RW])
        SLOT = 1032
        arena = sb("arena", [P, 21, SLOT])
        small = sb("small", [P, 64])
        xn = arena[:, 19:21, 0:D]
        gain_row = arena[:, 18, 0:D]
        rstd_diag = arena[:, 17, 0:T].rearrange("p (t n) -> p t n", t=2)
        rstd_row = arena[:, 17, T:2 * T]
        banks = ctx.enter_context(nc.psum_tensor("banks", [P, 8, 512], F32))

        def const(name, n=P):
            return cst[0:n, CONST_COLS[name]]

        def pcol(name, i=0, n=P, at=0):
            c = PARAM_COLS[name].start + i
            return par[at:at + n, c:c + 1]

        def c4(s):
            return arena[:, s, 0:4 * T].rearrange("p (j t) -> p j t", j=4)

        def flat(s, n=4 * T, m=P):
            return arena[0:m, s, 0:n]

        ident = const("ident")

        x_loaded = [sem("x_loaded_0"), sem("x_loaded_1")]
        ident_loaded, params_loaded = sem("ident_loaded"), sem("params_loaded")
        consts_loaded, gain_loaded = sem("consts_loaded"), sem("gain_loaded")
        block0_summed, warmed = sem("block0_summed"), sem("warmed")
        gu_landed = [sem("gu_landed_0"), sem("gu_landed_1")]
        dn_landed = [sem("dn_landed_0"), sem("dn_landed_1")]
        gu_hi_ready, gu_lo_ready = sem("gu_hi_ready"), sem("gu_lo_ready")
        dn_hi_ready, dn_lo_ready = sem("dn_hi_ready"), sem("dn_lo_ready")
        gu_used, dn_used = sem("gu_used"), sem("dn_used")
        gate_ready = sem("gate_ready")
        silu_ready, act_ready = sem("silu_ready"), sem("act_ready")
        act_hi_ready, act_lo_ready = sem("act_hi_ready"), sem("act_lo_ready")
        squares_ready, rstd_ready, xn_ready = sem("squares_ready"), sem("rstd_ready"), sem("xn_ready")
        xT_ready, h_hi_ready, h_lo_ready = sem("xT_ready"), sem("h_hi_ready"), sem("h_lo_ready")
        diag_ready, half_ready, row_summed, row_ready = (sem(n) for n in ("diag_ready", "half_ready", "row_summed",
                                                                          "row_ready"))
        eps_ready = sem("eps_ready")
        x_ready, stored = sem("x_ready"), sem("stored")

        def landed(eng, sems, pair, p):
            eng.wait_ge(sems[p], 16 * (pair + 1))

        def count(eng, s, value):
            if not isinstance(value, int) or value > 0:
                eng.wait_ge(s, value)

        def hi_gu(act, pair, p):
            landed(act, gu_landed, pair, p)
            count(act, gu_used, 2 * pair + p - 1)
            nc.scalar.copy(gu_hi[:, p, :], raw_gu[:, p, :]).then_inc(gu_hi_ready, 1)

        def hi_dn(act, pair, p, n=DN):
            landed(act, dn_landed, pair, p)
            count(act, dn_used, 2 * pair + p - 1)
            nc.scalar.copy(dn_hi[:, p, 0:n], raw_dn[:, p, 0:n]).then_inc(dn_hi_ready, 1)

        def lo_gu(dve, pair, p):
            dve.wait_ge(gu_hi_ready, 2 * pair + p + 1)
            nc.vector.tensor_tensor(gu_lo[:, p, :], raw_gu[:, p, :], gu_hi[:, p, :].bitcast(F32),
                                    ALU.subtract).then_inc(gu_lo_ready, 1)

        def lo_dn(dve, pair, p, n=DN):
            dve.wait_ge(dn_hi_ready, 2 * pair + p + 1)
            nc.vector.tensor_tensor(dn_lo[:, p, 0:n], raw_dn[:, p, 0:n], dn_hi[:, p, 0:n].bitcast(F32),
                                    ALU.subtract).then_inc(dn_lo_ready, 1)

        def lo_dn_pool(pool, pair, p):
            pool.wait_ge(dn_hi_ready, 2 * pair + p + 1)
            pool.wait_ge(dn_lo_ready, 2 * pair + p)
            nc.gpsimd.tensor_tensor(dn_lo[:, p, :], raw_dn[:, p, :], dn_hi[:, p, :].bitcast(F32),
                                    ALU.subtract).then_inc(dn_lo_ready, 1)

        def three_products(out, left, right, first, last):
            pairs = ((left[0], right[0]), (left[0], right[1]), (left[1], right[0]))
            for i, (a, b) in enumerate(pairs):
                ins = nc.tensor.matmul(out, a, b, start=first and i == 0, stop=last and i == 2)
            return ins

        def norm_act(act, s):
            rstd_of(act, s)
            h_hi_act(act, s)

        def h_hi_act(act, s):
            for b in range(4):
                act.wait_ge(xT_ready, 4 * s + b + 1)
                for i in range(2):
                    k = 2 * b + i
                    ins = nc.scalar.activation(h_hi[:, k, :], banks[:, b, i * T:(i + 1) * T], ACT.Copy,
                                               scale=pcol("norms", s * KD + k))
                ins.then_inc(h_hi_ready, 1)

        def rstd_of(act, s):
            squares_act(act, s, 0)
            squares_act(act, s, 1)
            inverse_root_act(act, s)

        def squares_act(act, s, t):
            if t == 0:
                nc.scalar.activation(warm[:, 0:1], eps_col[:, 0:1], ACT.Ln).then_inc(warmed, 1)
            if s == 0:
                act.wait_ge(x_loaded[t], 16)
            else:
                act.wait_ge(x_ready, 4 * s - 2 + 2 * t)
            nc.scalar.activation(xn[:, t, :], x[:, t, :], ACT.Square,
                                 accum_out=sumsq[:, t:t + 1]).then_inc(squares_ready, 1)

        def inverse_root_act(act, s):
            act.wait_ge(squares_ready, 2 * s + 2)
            nc.scalar.activation(rstd[:, :], sumsq[:, :], ACT.Ln, scale=1.0 / D, bias=eps_col[:, 0:1]
                                 ).then_inc(rstd_ready, 1)
            act.wait_ge(rstd_ready, 2 * s + 1)
            nc.scalar.activation(rstd[:, :], rstd[:, :], ACT.Exp, scale=-0.5).then_inc(rstd_ready, 1)

        def norm_dve(dve, s):
            dve.wait_ge(rstd_ready, 2 * s + 2)
            for t in range(2):
                nc.vector.tensor_scalar(xn[:, t, :], x[:, t, :], rstd[:, t:t + 1], None,
                                        ALU.mult).then_inc(xn_ready, 1)
            h_lo_dve(dve, s)

        def h_lo_dve(dve, s):
            for b in range(4):
                dve.wait_ge(h_hi_ready, 4 * s + b + 1)
                for i in range(2):
                    k = 2 * b + i
                    ins = nc.vector.scalar_tensor_tensor(
                        out=h_lo[:, k, :], in0=banks[:, b, i * T:(i + 1) * T], scalar=pcol("norms", s * KD + k),
                        in1=h_hi[:, k, :].bitcast(F32), op0=ALU.mult, op1=ALU.subtract)
                ins.then_inc(h_lo_ready, 1)

        def norm_pe(pe, s):
            for t in range(2):
                pe.wait_ge(xn_ready, 2 * sum(k != "ffn" for k in stages[:s]) + t + 1)
                for b in range(4):
                    for i in range(2):
                        ins = nc.tensor.transpose(banks[:, b, i * T + t * P:i * T + (t + 1) * P],
                                                  xn[:, t, (2 * b + i) * P:(2 * b + i + 1) * P], ident)
                    if t == 1:
                        ins.then_inc(xT_ready, 1)

        def gained_pe(pe, s):
            for t in range(2):
                for b in range(4):
                    if s == 0:
                        pe.wait_ge(x_loaded[t], 16)
                    elif b % 2 == 0:
                        pe.wait_ge(x_ready, 4 * s - 4 + 2 * t + b // 2 + 1)
                    for i in range(2):
                        ins = nc.tensor.transpose(banks[:, b, i * T + t * P:i * T + (t + 1) * P],
                                                  x[:, t, (2 * b + i) * P:(2 * b + i + 1) * P], ident)
                    if t == 1:
                        ins.then_inc(xT_ready, 1)

        def rstd_row_dve(dve, s):
            dve.wait_ge(rstd_ready, 2 * s + 2)
            nc.vector.tensor_scalar(rstd_half[:, :], rstd[:, :], 0.5, None, ALU.mult).then_inc(half_ready, 1)
            for t in range(2):
                ins = nc.vector.tensor_scalar(rstd_diag[:, t, :], ident, rstd[:, t:t + 1], None, ALU.mult)
            ins.then_inc(diag_ready, 1)

        def rstd_row_pe(pe, s):
            pe.wait_ge(diag_ready, ffn_index(s) + 1)
            for t in range(2):
                ins = nc.tensor.matmul(banks[:, 2, t * P:(t + 1) * P], const("ones"), rstd_diag[:, t, :], start=True, stop=True)
            ins.then_inc(row_summed, 1)

        def rstd_row_act(act, s):
            act.wait_ge(row_summed, ffn_index(s) + 1)
            nc.scalar.copy(rstd_row, banks[:, 2, 0:T]).then_inc(row_ready, 1)

        def ffn_index(s):
            return sum(k == "ffn" for k in stages[:s])

        def add_to_x(dve, s):
            if s + 1 < len(stages):
                lo_gu(dve, first_pair[s + 1], 0)
            if stages[s] == "ffn":
                dve.wait_ge(half_ready, ffn_index(s) + 1)
            for t in range(2):
                if t == 0:
                    dve.wait_ge(block0_summed, s + 1)
                else:
                    dve.wait_ge(dn_used if stages[s] == "ffn" else gu_used, last_unit[s])
                for c in range(2):
                    nc.vector.scalar_tensor_tensor(
                        out=x[:, t, c * 512:(c + 1) * 512], in0=banks[:, 4 + 2 * t + c, :],
                        scalar=rstd_half[:, t:t + 1] if stages[s] == "ffn" else 1.0,
                        in1=x[:, t, c * 512:(c + 1) * 512], op0=ALU.mult, op1=ALU.add).then_inc(x_ready, 1)

        def first_lo_gu(dve, s):
            if s == 0:
                lo_gu(dve, 0, 0)

        def ffn_act(act, pair, p, f, ahead):
            hi_dn(act, pair, p)
            act.wait_ge(gate_ready, f + 1)
            nc.scalar.activation(silu[:, p, :], silu[:, p, :], ACT.Silu).then_inc(silu_ready, 1)
            act.wait_ge(act_ready, f + 1)
            nc.scalar.copy(act_hi[:, p, :], act32[:, p, :]).then_inc(act_hi_ready, 1)
            if ahead:
                hi_gu(act, pair + 1, p)

        def ffn_dve(dve, pair, p, f, ahead):
            dve.wait_ge(gu_used, 2 * pair + p + 1)
            nc.vector.tensor_tensor(silu[:, p, :], banks[:, p, 0:T], rstd_row, ALU.mult).then_inc(gate_ready, 1)
            lo_dn(dve, pair, p)
            dve.wait_ge(silu_ready, f + 1)
            nc.vector.tensor_tensor(act32[:, p, :], silu[:, p, :], banks[:, p, T:2 * T],
                                    ALU.mult).then_inc(act_ready, 1)
            dve.wait_ge(act_hi_ready, f + 1)
            nc.vector.tensor_tensor(act_lo[:, p, :], act32[:, p, :], act_hi[:, p, :].bitcast(F32),
                                    ALU.subtract).then_inc(act_lo_ready, 1)
            if ahead:
                lo_gu(dve, pair + 1, p)

        def ffn_up(pe, pair, p, f, norm=None):
            pe.wait_ge(gu_lo_ready, 2 * pair + p + 1)
            count(pe, act_ready, f - 1)
            for side in range(2):
                for k in range(KD):
                    if norm is not None and side == 0 and k % 2 == 0:
                        pe.wait_ge(h_lo_ready, 4 * norm + k // 2 + 1)
                    w = slice((side * KD + k) * P, (side * KD + k + 1) * P)
                    ins = three_products(banks[:, p, side * T:(side + 1) * T],
                                         (gu_hi[:, p, w], gu_lo[:, p, w]), (h_hi[:, k, :], h_lo[:, k, :]),
                                         k == 0, k == KD - 1)
            ins.then_inc(gu_used, 1)

        def ffn_down(pe, pair, p, f, first, last):
            pe.wait_ge(dn_lo_ready, 2 * pair + p + 1)
            pe.wait_ge(act_lo_ready, f + 1)
            for t in range(2):
                tok = slice(t * P, (t + 1) * P)
                for c in range(2):
                    w = slice(c * 512, (c + 1) * 512)
                    ins = three_products(banks[:, 4 + 2 * t + c, :], (act_hi[:, p, tok], act_lo[:, p, tok]),
                                         (dn_hi[:, p, w], dn_lo[:, p, w]), first, last)
                if last and t == 0:
                    ins.then_inc(block0_summed, 1)
            ins.then_inc(dn_used, 1)

        def ffn_number(s):
            return FFN_UNITS * sum(k == "ffn" for k in stages[:s])

        HALF = FFN_UNITS // 2

        def ffn_all_act(act, s):
            b, f = first_pair[s], ffn_number(s)
            early = 0 if s == 0 else 2 if stages[s - 1] == "ffn" else 1
            for p in range(early):
                hi_gu(act, b, p)
            squares = (1,) if s else (0, 1)
            if s:
                squares_act(act, s, 0)
            h_hi_act(act, s)
            for t in squares:
                squares_act(act, s, t)
            inverse_root_act(act, s)
            for p in range(early, 2):
                hi_gu(act, b, p)
            rstd_row_act(act, s)
            first = 0
            if b == 0:
                ffn_act(act, 0, 0, 0, True)
                ffn_act(act, 0, 1, 1, True)
                first = 1
            with act.Fori(first, HALF - 1) as i:
                ffn_act(act, b + i, 0, f + 2 * i, True)
                ffn_act(act, b + i, 1, f + 2 * i + 1, True)
            i = HALF - 1
            ffn_act(act, b + i, 0, f + 2 * i, False)
            ffn_act(act, b + i, 1, f + 2 * i + 1, False)

        def ffn_all_dve(dve, s):
            b, f = first_pair[s], ffn_number(s)
            h_lo_dve(dve, s)
            if s > 0 and stages[s - 1] == "ffn":
                lo_gu(dve, b, 1)
                rstd_row_dve(dve, s)
            else:
                rstd_row_dve(dve, s)
                first_lo_gu(dve, s)
                lo_gu(dve, b, 1)
            dve.wait_ge(row_ready, ffn_index(s) + 1)
            first = 0
            if b == 0:
                ffn_dve(dve, 0, 0, 0, True)
                ffn_dve(dve, 0, 1, 1, True)
                first = 1
            with dve.Fori(first, HALF - 1) as i:
                ffn_dve(dve, b + i, 0, f + 2 * i, True)
                ffn_dve(dve, b + i, 1, f + 2 * i + 1, True)
            i = HALF - 1
            ffn_dve(dve, b + i, 0, f + 2 * i, False)
            ffn_dve(dve, b + i, 1, f + 2 * i + 1, False)
            add_to_x(dve, s)

        def ffn_all_pe(pe, s):
            b, f = first_pair[s], ffn_number(s)
            gained_pe(pe, s)
            ffn_up(pe, b, 0, f, s)
            rstd_row_pe(pe, s)
            ffn_up(pe, b, 1, f + 1)
            ffn_down(pe, b, 0, f, True, False)
            with pe.Fori(0, HALF - 1) as i:
                ffn_up(pe, b + 1 + i, 0, f + 2 + 2 * i)
                ffn_down(pe, b + i, 1, f + 1 + 2 * i, False, False)
                ffn_up(pe, b + 1 + i, 1, f + 3 + 2 * i)
                ffn_down(pe, b + 1 + i, 0, f + 2 + 2 * i, False, False)
            ffn_down(pe, b + HALF - 1, 1, f + FFN_UNITS - 1, False, True)

        def unit(s, u):
            return first_pair[s] + u // 2, u % 2

        def split_act(act, s, u, n=DN):
            if 2 * first_pair[s] + u + 1 < last_unit[s]:
                hi_gu(act, *unit(s, u + 1))
            hi_dn(act, *unit(s, u), n)

        def split_dve(dve, s, u, n=DN):
            if 2 * first_pair[s] + u + 1 < last_unit[s]:
                lo_gu(dve, *unit(s, u + 1))
            lo_dn(dve, *unit(s, u), n)

        def gu_weights(pe, s, u):
            pair, p = unit(s, u)
            pe.wait_ge(gu_lo_ready, 2 * pair + p + 1)
            return lambda a, n: (gu_hi[:, p, a:a + n], gu_lo[:, p, a:a + n])

        def dn_weights(pe, s, u):
            pair, p = unit(s, u)
            pe.wait_ge(dn_lo_ready, 2 * pair + p + 1)
            return lambda a, n: (dn_hi[:, p, a:a + n], dn_lo[:, p, a:a + n])

        def channel_tile(out, w, base, m=P, norm=None):
            for k in range(KD):
                if norm is not None and k % 2 == 0:
                    nc.tensor.wait_ge(h_lo_ready, 4 * norm + k // 2 + 1)
                ins = three_products(out, w(base + k * m, m), (h_hi[:, k, :], h_lo[:, k, :]), k == 0, k == KD - 1)
            return ins

        def w_out_pe(pe, s, u0, ks, ready=None, turn=0):
            for k in ks:
                i, place = divmod(k, 3)
                w = (dn_weights if place == 2 else gu_weights)(pe, s, u0 + i)
                base = D if place == 1 else 0
                if ready:
                    ready(k)
                for t in range(2):
                    for c in range(2):
                        ins = three_products(banks[:, 4 + 2 * t + c, :],
                                             (h_hi[:, (k + turn) % KD, t * P:(t + 1) * P],
                                              h_lo[:, (k + turn) % KD, t * P:(t + 1) * P]),
                                             w(base + c * 512, 512), k == 0, k == KD - 1)
                    if k == KD - 1 and t == 0:
                        ins.then_inc(block0_summed, 1)
                if k == KD - 1:
                    dn_weights(pe, s, u0 + i)
                if place == 2 or k == KD - 2:
                    ins.then_inc(dn_used, 1)
                elif place == 1:
                    ins.then_inc(gu_used, 1)

        def part_used(eng, s, u, part):
            eng.wait_ge((gu_used, dn_used)[part], 2 * first_pair[s] + u + 1)

        def eye_view(name, n):
            return const(name).rearrange("p (o t) -> p o t", o=1).to_broadcast([P, n, P])

        R_, K_, V_, LOW, CB, CC, CU, TMP, SW, AI, GATE, CS, E1, KKN, AT_, RT_, BT_, KT_, BV, RST, YC = range(21)
        A_TOK, B_TOK, K_TOK, V_TOK = R_, K_, LOW, TMP
        AB, MI, MT, XB, AO, G2, PHI, DD, ST = SW, AI, CS, E1, KKN, RST, CB, CC, CU
        NL = len(LEVELS)
        CONV = ("u", "tap0", "tap1", "tap2", "y_conv")

        def order(*parts):
            return [n for part in parts for n in (part if isinstance(part, list) else [part])]

        def even_names():
            pe = order([("tile", i) for i in (0, 3, 6, 9, 14)], "decay_in", "iclr_in", ("tile", 17), "gate_in", "key_norm",
                       ("tile", 20), ("tile", 23), "bonus",
                       [("tok", a) for a in "abkv"])
            for jj in range(2):
                pe += order(("ab", jj), ("m", jj), ("ak", jj))
                for l in range(NL):
                    pe += [(n, jj, l, g) for n in ("x", "mt", "m")[:3 if l < NL - 1 else 2] for g in range(2)]
                pe += order(*[(n, jj) for n in ("rb", "rk", "g", "uw", "y0", "q", "phi", "d")])
            pe += order(("phi_s", 1), ("y_s", 1), ("phi_s", 2), ("y_s", 2), ("y_s", 3), "mean", "var")
            act = order([("evac", i) for i in range(14)], "tanh", "gate_sig", [("evac", i) for i in (14, 15, 16)],
                        "decay_sig", "iclr", "square_k", [("evac", i) for i in (17, 18, 19)], "gate", "e0", "e1", "em",
                        "ln_k", "inv_k", [("evac", i) for i in range(20, 26)],
                        [("tok", a) for a in "abkv"])
            for jj in range(2):
                act += [("m", jj)]
                act += [(n, jj, l, g) for l in range(NL) for n in ("x", "m")[:2 if l < NL - 1 else 1] for g in range(2)]
                act += ["y_conv_hi"] * (jj == 0) + [(n, jj) for n in ("g", "uw", "y0", "phi")]
            act += order("square_y", "ln_y", "rstd_y", [("y_hi", j) for j in range(4)])
            dve = order([(n, a) for a in "rkv" for n in ("diff", "mix")], ("diff", "l"), ("mix", "l"), "omka", "kkn0",
                        "scan", "csx", "key_ss", "kkn", "b", "at", "bt", "factor", "kh", "kt", "rt", "ec", "bonus", "bv")
            for jj in range(2):
                dve += order(("ab", jj), ("mt0", jj), ("mt1", jj)) + ["y_conv_lo", "bv_b"] * (jj == 1)
                for l in range(NL):
                    dve += [("mt", jj, l, g) for g in range(2)] + [CONV[l]] * (jj == 0)
                dve += order(*[(n, jj) for n in ("ak", "rb", "rk", "q", "d")])
            dve += order("s1", ("bd", 1))
            for n in (1, 2):
                dve += order(("sd", n), ("sum", n), ("s", n), ("y", n), ("bd", n + 1))
            dve += order(("y", 3), "centred")
            for j in range(5):
                dve += [(n, j) for n in ("normed", "affine", "gated")] * (j < 4) + [("y_lo", j - 1)] * (j > 0)
            pool = order("pads", "reset1", "reset0", [("ao", 0, l) for l in range(NL)], "phi0", "bd0",
                         [("ao", 1, l) for l in range(NL)])
            return pe, act, dve, pool

        def padded(slot, w):
            return arena[:, slot, 0:4 * w].rearrange("p (j t) -> p j t", j=4)

        def low(m, i):
            return arena[0:m, LOW, i * 257:(i + 1) * 257]

        def tok(slot):
            return arena[:, slot, 0:1024].rearrange("p (j m c) -> p j m c", j=4, m=2)

        def prob(slot):
            return arena[:, slot, 0:1024].rearrange("p (g j m t) -> p g j m t", g=2, j=2, m=2)

        phi = arena[:, PHI, 0:1024].rearrange("p (j n t) -> p j n t", j=4, n=2)
        dd = arena[:, DD, 0:768].rearrange("p (j n t) -> p j n t", j=4, n=3)
        state = arena[:, ST, 0:256].rearrange("p (j t) -> p j t", j=4)
        state_sum = arena[:, ST, 768:1024].rearrange("p (j t) -> p j t", j=4)
        state_bd = arena[:, ST, 256:768].rearrange("p (j t) -> p j t", j=4)
        ec = small[:, 0:16].rearrange("p (j n) -> p j n", j=4)
        omka = small[:, 16:20]

        def rows64(g):
            return slice(64 * g, 64 * g + 64)

        EV = {}
        if "even" in stages:
            for eng, names in zip(("pe", "act", "dve", "pool"), even_names()):
                EV[eng] = Steps(sem(f"rwkv_{eng}_steps"), names)

        def after(eng, who, name):
            if who == "pe" and name[0] == "tile":
                s, i = stages.index("even"), name[1]
                c = i if i < 12 else i + 1
                u, r = (4, 3 - (i - 11)) if i in (12, 13) else divmod(c, 3)
                if r:
                    part_used(eng, s, u, r - 1)
                    return
            eng.wait_ge(EV[who].sem, EV[who].value[name])

        def even_pool(pool, s):
            done = EV["pool"].done
            for slot in (R_, K_, V_):
                nc.gpsimd.memset(padded(slot, 257)[:, :, 0:1], 0.0)
            for i in range(2):
                nc.gpsimd.memset(low(P, i)[:, 0:1], 0.0)
            done(nc.gpsimd.memset(padded(CU, 258)[:, :, 0:2], 0.0), "pads")
            pool.wait_ge(xT_ready, 4 * s + 4)
            done(nc.gpsimd.memset(flat(RST), 1.0), "reset1")
            after(pool, "pool", "reset1")
            done(nc.gpsimd.memset(flat(RST).rearrange("p (n c) -> p n c", c=CHUNK)[:, :, 0:1], 0.0), "reset0")
            for u in range(5, 11):
                lo_dn_pool(pool, *unit(s, u))
            for jj in range(2):
                if jj == 1:
                    after(pool, "dve", "y_conv")
                    done(nc.gpsimd.memset(flat(PHI), 0.0), "phi0")
                    done(nc.gpsimd.memset(arena[:, ST, 256:768], 0.0), "bd0")
                after(pool, "dve", ("ab", jj))
                for l, n in enumerate(LEVELS):
                    if l:
                        after(pool, "pe", ("x", jj, l - 1, 1))
                    done(nc.gpsimd.tensor_tensor(flat(AO).rearrange("p (q t) -> p q t", t=P),
                                                 flat(AB).rearrange("p (q t) -> p q t", t=P),
                                                 eye_view(f"join{n}", 8), ALU.mult), ("ao", jj, l))

        def even_act(act, s):
            done = EV["act"].done

            def evac(i):
                after(act, "pe", ("tile", i))
                src = banks[:, i % 4, 0:T]
                if i < 12:
                    dst = padded((R_, K_, V_)[i // 4], 257)[:, i % 4, 1:257]
                elif i < 14:
                    m = (64, GATE_RANK)[i - 12]
                    dst, src = low(m, i - 12)[:, 1:257], banks[0:m, i % 4, 0:T]
                else:
                    c, j = divmod(i - 14, 4)
                    dst = padded(CU, 258)[:, j, 2:258] if c == 2 else c4((CB, CC)[c])[:, j, :]
                done(nc.scalar.copy(dst, src), ("evac", i))

            hi_gu(act, *unit(s, 0))
            norm_act(act, s)
            for u in range(4):
                split_act(act, s, u)
                for i in range(3 * u, 3 * u + 3):
                    evac(i)
            split_act(act, s, 4, 64)
            evac(12)
            evac(13)
            split_act(act, s, 5)
            after(act, "dve", ("mix", "l"))
            m = DECAY_RANK
            done(nc.scalar.activation(low(m, 0)[:, 1:257], low(m, 0)[:, 1:257], ACT.Tanh), "tanh")
            m = GATE_RANK
            done(nc.scalar.activation(low(m, 1)[:, 1:257], low(m, 1)[:, 1:257], ACT.Sigmoid), "gate_sig")
            for i in (14, 15, 16):
                evac(i)
            for name, first, slot, bias in (("decay_in", 4, SW, "w0"), ("iclr_in", 6, AI, "a0")):
                after(act, "pe", name)
                for j in range(4):
                    ins = nc.scalar.activation(c4(slot)[:, j, :], banks[:, first + j // 2, (j % 2) * T:(j % 2 + 1) * T],
                                               ACT.Sigmoid, bias=pcol(bias, j))
                done(ins, "decay_sig" if name == "decay_in" else "iclr")
            after(act, "dve", "kkn0")
            done(nc.scalar.activation(flat(YC), flat(KKN), ACT.Square), "square_k")
            split_act(act, s, 6)
            hi_dn(act, *unit(s, 7))
            for i in (17, 18, 19):
                evac(i)
            hi_gu(act, *unit(s, 8))
            hi_dn(act, *unit(s, 8))
            after(act, "pe", "gate_in")
            done(nc.scalar.copy(flat(GATE).rearrange("p (b n) -> p b n", b=2), banks[:, 4:6, :]), "gate")
            after(act, "dve", "csx")
            done(nc.scalar.activation(flat(SW), flat(SW), ACT.Exp, scale=-LOG_W), "e0")
            done(nc.scalar.activation(flat(E1), flat(CS), ACT.Exp, scale=-LOG_W), "e1")
            done(nc.scalar.activation(flat(CS), flat(CS), ACT.Exp, scale=LOG_W), "em")
            after(act, "dve", "key_ss")
            done(nc.scalar.activation(flat(TMP), flat(TMP), ACT.Ln, scale=float(2 ** KK_SHIFT)), "ln_k")
            after(act, "act", "ln_k")
            done(nc.scalar.activation(flat(TMP), flat(TMP), ACT.Exp, scale=-0.5, bias=eps_col[:, 2:3]), "inv_k")
            for i in (20, 21, 22):
                evac(i)
            hi_gu(act, *unit(s, 9))
            for i in (23, 24, 25):
                evac(i)
            split_act(act, s, 9)
            hi_dn(act, *unit(s, 10))
            after(act, "dve", "bv")
            for name, slot, b in (("a", A_TOK, 0), ("b", B_TOK, 2), ("k", K_TOK, 4), ("v", V_TOK, 6)):
                after(act, "pe", ("tok", name))
                done(nc.scalar.copy(flat(slot).rearrange("p (b n) -> p b n", b=2), banks[:, b:b + 2, :]), ("tok", name))
            for jj in range(2):
                after(act, "pe", ("m", jj))
                done(nc.scalar.copy(flat(MI).rearrange("p (b n) -> p b n", b=2), banks[:, 2:4, :]), ("m", jj))
                for l in range(NL):
                    for g in range(2):
                        after(act, "pe", ("x", jj, l, g))
                        if l:
                            after(act, "pe", ("mt", jj, l - 1, g))
                        done(nc.scalar.copy(arena[:, XB, g * 512:(g + 1) * 512], banks[:, 4 + g, :]), ("x", jj, l, g))
                    if l < NL - 1:
                        for g in range(2):
                            after(act, "pe", ("m", jj, l, g))
                            done(nc.scalar.copy(arena[:, MI, g * 512:(g + 1) * 512], banks[:, 2 + g, :]), ("m", jj, l, g))
                if jj == 0:
                    after(act, "dve", "y_conv")
                    after(act, "pe", ("tile", 25))
                    done(nc.scalar.copy(h_hi[:, 0:4, :], c4(YC)), "y_conv_hi")
                after(act, "pe", ("g", jj))
                done(nc.scalar.copy(arena[:, G2, 0:512], banks[:, 0, :]), ("g", jj))
                after(act, "pe", ("uw", jj))
                done(nc.scalar.copy(flat(MI).rearrange("p (b n) -> p b n", b=2), banks[:, 6:8, :]), ("uw", jj))
                after(act, "pe", ("y0", jj))
                done(nc.scalar.copy(arena[:, AT_, jj * 512:(jj + 1) * 512], banks[:, 1, :]), ("y0", jj))
                after(act, "pe", ("phi", jj))
                if jj == 0:
                    after(act, "pool", "phi0")
                for g in range(2):
                    for n in (1, 2):
                        r = rows64(g)
                        src = banks[r, 3 if n == 1 else 2, 0:128].rearrange("p (j t) -> p j t", j=2)
                        ins = nc.scalar.copy(phi[r, 2 * jj:2 * jj + 2, n - 1, r], src)
                done(ins, ("phi", jj))
            hi_gu(act, *unit(s, 11))
            hi_dn(act, *unit(s, 11), 64)
            after(act, "dve", "centred")
            done(nc.scalar.activation(flat(A_TOK), flat(AT_), ACT.Square), "square_y")
            after(act, "pe", "var")
            done(nc.scalar.activation(flat(B_TOK).rearrange("p (b n) -> p b n", b=2), banks[:, 2:4, :], ACT.Ln,
                                      scale=1.0 / 64, bias=eps_col[:, 1:2]), "ln_y")
            after(act, "act", "ln_y")
            done(nc.scalar.activation(flat(B_TOK), flat(B_TOK), ACT.Exp, scale=-0.5), "rstd_y")
            for j in range(4):
                after(act, "dve", ("gated", j))
                done(nc.scalar.copy(h_hi[:, 4 + j, :], c4(AT_)[:, j, :]), ("y_hi", j))

        def even_dve(dve, s):
            def done(ins, name):
                EV["dve"].done(ins, name)
                dve.wait_ge(EV["dve"].sem, EV["dve"].finished)

            tt, ts, stt = nc.vector.tensor_tensor, nc.vector.tensor_scalar, nc.vector.scalar_tensor_tensor

            def token_mix(name, slot, col):
                v = padded(slot, 257)
                done(tt(c4(TMP), v[:, :, 0:T], v[:, :, 1:257], ALU.subtract), ("diff", name))
                for j in range(4):
                    ins = stt(out=v[:, j, 1:257], in0=c4(TMP)[:, j, :], scalar=pcol("mu", col + j),
                              in1=v[:, j, 1:257], op0=ALU.mult, op1=ALU.add)
                done(ins, ("mix", name))

            first_lo_gu(dve, s)
            norm_dve(dve, s)
            split_dve(dve, s, 0)
            after(dve, "pool", "pads")
            for u, name, slot in ((1, "r", R_), (2, "k", K_), (3, "v", V_)):
                split_dve(dve, s, u)
                after(dve, "act", ("evac", 4 * u - 1))
                token_mix(name, slot, 4 * (u - 1))
            split_dve(dve, s, 4, 64)
            after(dve, "act", ("evac", 13))
            for i, m in ((0, 64), (1, GATE_RANK)):
                ins = tt(c4(TMP)[0:m, i, :], low(m, i)[:, 0:T], low(m, i)[:, 1:257], ALU.subtract)
            done(ins, ("diff", "l"))
            for i, m in ((0, 64), (1, GATE_RANK)):
                ins = stt(out=low(m, i)[:, 1:257], in0=c4(TMP)[0:m, i, :], scalar=pcol("mu", 12 + i, m),
                          in1=low(m, i)[:, 1:257], op0=ALU.mult, op1=ALU.add)
            done(ins, ("mix", "l"))
            lo_gu(dve, *unit(s, 6))
            k, r = padded(K_, 257)[:, :, 1:257], padded(R_, 257)[:, :, 1:257]
            v = padded(V_, 257)[:, :, 1:257]
            ka = PARAM_COLS["k_a"]
            done(ts(omka, par[:, ka], -1.0, 1.0, ALU.mult, ALU.add), "omka")
            for j in range(4):
                ins = ts(c4(KKN)[:, j, :], k[:, j, :], pcol("k_k", j), None, ALU.mult)
            done(ins, "kkn0")
            lo_gu(dve, *unit(s, 7))
            after(dve, "act", "decay_sig")
            after(dve, "pool", "reset0")
            done(nc.vector.tensor_tensor_scan(flat(CS), flat(RST), flat(SW), 0.0, ALU.mult, ALU.add), "scan")
            done(tt(flat(SW), flat(CS), flat(SW), ALU.subtract), "csx")
            lo_gu(dve, *unit(s, 8))
            after(dve, "pe", "key_norm")
            done(ts(flat(TMP).rearrange("p (b n) -> p b n", b=2), banks[:, 6:8, :], 1e-24, None, ALU.max), "key_ss")
            after(dve, "act", "inv_k")
            done(tt(flat(KKN), flat(KKN), flat(TMP), ALU.mult), "kkn")
            done(tt(flat(BT_), flat(KKN), flat(AI), ALU.mult), "b")
            done(stt(out=flat(AT_), in0=flat(KKN), scalar=-1.0, in1=flat(SW), op0=ALU.mult, op1=ALU.mult), "at")
            done(tt(flat(BT_), flat(BT_), flat(CS), ALU.mult), "bt")
            for j in range(4):
                ins = ts(c4(TMP)[:, j, :], c4(AI)[:, j, :], pcol("k_a", j), omka[:, j:j + 1], ALU.mult, ALU.add)
            done(ins, "factor")
            done(tt(c4(RST), c4(TMP), k, ALU.mult), "kh")
            done(tt(flat(KT_), flat(RST), flat(CS), ALU.mult), "kt")
            done(tt(c4(RT_), r, c4(E1), ALU.mult), "rt")
            done(nc.vector.tensor_copy(ec, flat(E1).rearrange("p (j n c) -> p j n c", j=4, c=CHUNK)[:, :, :, CHUNK - 1]),
                 "ec")
            for j in range(4):
                ins = stt(out=c4(TMP)[:, j, :], in0=r[:, j, :], scalar=pcol("r_k", j), in1=c4(RST)[:, j, :],
                          op0=ALU.mult, op1=ALU.mult)
            done(ins, "bonus")
            after(dve, "pe", "bonus")
            bv = flat(BV).rearrange("p (b i t) -> p b i t", b=2, i=2)
            done(tt(bv, banks[:, 6:8, :].rearrange("p b (i t) -> p b i t", i=2),
                    v.rearrange("p (b i) t -> p b i t", b=2), ALU.mult), "bv")
            lo_gu(dve, *unit(s, 9))
            lo_gu(dve, *unit(s, 10))
            def convolution(step):
                u = padded(CU, 258)
                if step == "u":
                    after(dve, "act", ("evac", 25))
                    ins = tt(u[:, :, 2:258], c4(CC), u[:, :, 2:258], ALU.mult)
                elif step == "y_conv":
                    ins = tt(flat(YC), flat(CB), flat(CC), ALU.mult)
                else:
                    tap = int(step[3:])
                    for j in range(4):
                        w = pcol("conv_w", 4 * tap + j)
                        if tap == 0:
                            ins = ts(c4(CC)[:, j, :], u[:, j, 0:T], w, None, ALU.mult)
                        else:
                            ins = stt(out=c4(CC)[:, j, :], in0=u[:, j, tap:tap + T], scalar=w, in1=c4(CC)[:, j, :],
                                      op0=ALU.mult, op1=ALU.add)
                done(ins, step)

            def masked(slot, b, mask, name, jj):
                after(dve, "pe", (name, jj))
                done(tt(flat(slot).rearrange("p (b q t) -> p b q t", b=2, t=P),
                        banks[:, b:b + 2, :].rearrange("p b (q t) -> p b q t", t=P),
                        const(mask).rearrange("p (b q t) -> p b q t", b=1, q=1).to_broadcast([P, 2, 4, P]),
                        ALU.mult), (name, jj))

            eight = lambda slot: flat(slot).rearrange("p (q t) -> p q t", t=P)
            for jj in range(2):
                masked(AB, 0, "before", "ab", jj)
                done(tt(eight(MT), eight(AB), eye_view("pairs", 8), ALU.mult), ("mt0", jj))
                done(tt(eight(MT), eight(MT), eye_view("ident", 8), ALU.add), ("mt1", jj))
                if jj == 1:
                    after(dve, "act", "y_conv_hi")
                    done(tt(h_lo[:, 0:4, :], c4(YC), h_hi[:, 0:4, :].bitcast(F32), ALU.subtract), "y_conv_lo")
                    for j in range(4):
                        ins = ts(c4(BV)[:, j, :], c4(BV)[:, j, :], pcol("ln_b", j), None, ALU.add)
                    done(ins, "bv_b")
                for l in range(NL):
                    for g in range(2):
                        half = slice(g * 512, (g + 1) * 512)
                        after(dve, "pe", ("mt", jj, l, g))
                        done(tt(arena[:, MT, half], arena[:, MT, half], banks[:, 6 + g, :], ALU.add), ("mt", jj, l, g))
                    if jj == 0:
                        convolution(CONV[l])
                after(dve, "pool", ("ao", jj, NL - 1))
                masked(AB, 0, "before", "ak", jj)
                masked(XB, 4, "not_after", "rb", jj)
                masked(AO, 2, "not_after", "rk", jj)
                after(dve, "pe", ("q", jj))
                rt = arena[:, RT_, jj * 512:(jj + 1) * 512]
                done(tt(rt, rt, banks[:, 5, :], ALU.add), ("q", jj))
                after(dve, "pe", ("d", jj))
                if jj == 0:
                    after(dve, "pool", "bd0")
                nc.vector.tensor_copy(dd[:, 2 * jj:2 * jj + 2, 0:3:2, :],
                                      banks[:, 4, 0:256].rearrange("p (j n t) -> p j n t", j=2, n=2))
                done(nc.vector.tensor_copy(dd[:, 2 * jj:2 * jj + 2, 1, :],
                                           banks[:, 7, 0:128].rearrange("p (j t) -> p j t", j=2)), ("d", jj))

            def decay_end(n):
                return ec[:, :, n:n + 1].to_broadcast([P, 4, 64])

            def block_diagonal(n):
                for g in range(2):
                    ins = nc.vector.tensor_copy(state_bd[rows64(g), :, rows64(g)], state[rows64(g), :, :])
                done(ins, ("bd", n))

            done(tt(state, dd[:, :, 0, :], decay_end(0), ALU.mult), "s1")
            block_diagonal(1)

            def add_y(n):
                after(dve, "pe", ("y_s", n))
                y = c4(AT_)[:, :, n * CHUNK:(n + 1) * CHUNK]
                done(tt(y, y, banks[:, 2 + (n - 1) % 2, 0:256].rearrange("p (j t) -> p j t", j=4), ALU.add), ("y", n))

            after(dve, "act", ("y0", 1))
            for n in (1, 2):
                done(tt(state_sum, state, dd[:, :, n, :], ALU.add), ("sd", n))
                after(dve, "pe", ("phi_s", n))
                done(tt(state_sum, state_sum, banks[:, n - 1, 0:256].rearrange("p (j t) -> p j t", j=4), ALU.add),
                     ("sum", n))
                done(tt(state, state_sum, decay_end(n), ALU.mult), ("s", n))
                add_y(n)
                block_diagonal(n + 1)
            add_y(3)
            two = lambda slot: flat(slot).rearrange("p (b n) -> p b n", b=2)
            after(dve, "pe", "mean")
            done(stt(out=two(AT_), in0=banks[:, 0:2, :], scalar=-1.0 / 64, in1=two(AT_), op0=ALU.mult, op1=ALU.add),
                 "centred")
            lo_gu(dve, *unit(s, 11))
            dve.wait_ge(dn_lo_ready, 2 * first_pair[s] + 11)
            lo_dn(dve, *unit(s, 11), 64)
            after(dve, "act", "rstd_y")
            y = c4(AT_)
            for j in range(5):
                if j < 4:
                    done(tt(y[:, j, :], y[:, j, :], c4(B_TOK)[:, j, :], ALU.mult), ("normed", j))
                    done(stt(out=y[:, j, :], in0=y[:, j, :], scalar=pcol("ln_w", j), in1=c4(BV)[:, j, :],
                             op0=ALU.mult, op1=ALU.add), ("affine", j))
                    done(tt(y[:, j, :], y[:, j, :], c4(GATE)[:, j, :], ALU.mult), ("gated", j))
                if j > 0:
                    after(dve, "act", ("y_hi", j - 1))
                    done(tt(h_lo[:, 3 + j, :], y[:, j - 1, :], h_hi[:, 3 + j, :].bitcast(F32), ALU.subtract),
                         ("y_lo", j - 1))
            add_to_x(dve, s)

        def even_pe(pe, s):
            done = EV["pe"].done
            mm = nc.tensor.matmul
            norm_pe(pe, s)

            def tiles(u, first):
                for part in range(2):
                    w = (gu_weights, dn_weights)[part](pe, s, u)
                    for i in ((first, first + 1), (first + 2,))[part]:
                        if i >= 4:
                            after(pe, "act", ("evac", i - 4))
                        ins = channel_tile(banks[:, i % 4, 0:T], w, (i - first) * DN if part == 0 else 0,
                                           norm=s if i == 0 else None)
                        if i == first:
                            done(ins, ("tile", i))
                    ins.then_inc((gu_used, dn_used)[part], 1)

            for u in range(4):
                tiles(u, 3 * u)
            w = gu_weights(pe, s, 4)
            dn_weights(pe, s, 4)
            for i, base, m, used in ((12, 0, 64, dn_used), (13, 512, GATE_RANK, gu_used)):
                after(pe, "act", ("evac", i - 4))
                channel_tile(banks[0:m, i % 4, 0:T], w, base, m).then_inc(used, 1)
            tiles(5, 14)

            def low_rank(name, first, m, row, i):
                for j in range(4):
                    ins = mm(banks[:, first + j // 2, (j % 2) * T:(j % 2 + 1) * T],
                             lora[row:row + m, i, j * P:(j + 1) * P],
                             arena[row:row + m, LOW, i * 257 + 1:i * 257 + 257], start=True, stop=True)
                done(ins, name)

            after(pe, "act", "tanh")
            low_rank("decay_in", 4, DECAY_RANK, 0, 0)
            low_rank("iclr_in", 6, ICLR_RANK, DECAY_RANK, 0)
            tiles(6, 17)
            after(pe, "act", "gate_sig")
            after(pe, "act", "decay_sig")
            low_rank("gate_in", 4, GATE_RANK, 0, 1)

            def over_heads(name, slot, first):
                for b in range(2):
                    ins = mm(banks[:, first + b, :], const("head_ones"), arena[:, slot, b * 512:(b + 1) * 512],
                             start=True, stop=True)
                done(ins, name)

            after(pe, "act", "iclr")
            after(pe, "act", "square_k")
            over_heads("key_norm", YC, 6)
            tiles(7, 20)
            tiles(8, 23)
            after(pe, "dve", "key_ss")
            after(pe, "dve", "bonus")
            over_heads("bonus", TMP, 6)
            after(pe, "act", ("evac", 25))
            after(pe, "act", "gate")
            for name, src, b in (("a", c4(AT_), 0), ("b", c4(BT_), 2), ("k", c4(KT_), 4),
                                 ("v", padded(V_, 257)[:, :, 1:257], 6)):
                if name == "v":
                    after(pe, "dve", "bv")
                for j in range(4):
                    for m in range(2):
                        ins = nc.tensor.transpose(banks[:, b + j // 2, (j % 2 * 2 + m) * P:(j % 2 * 2 + m + 1) * P],
                                                  src[:, j, m * P:(m + 1) * P], ident)
                done(ins, ("tok", name))

            def each(g):
                return [(jl, m, (jl * 2 + m) * P) for jl in range(2) for m in range(2)]

            def scores(name, jj, left, right, b):
                for g in range(2):
                    for jl, m, at in each(g):
                        t = slice(m * P, (m + 1) * P)
                        ins = mm(banks[:, b + g, at:at + P], c4(left)[rows64(g), 2 * jj + jl, t],
                                 c4(right)[rows64(g), 2 * jj + jl, t], start=True, stop=True)
                done(ins, (name, jj))

            for jj in range(2):
                ab, mi, mt, xb, ao = (prob(x_) for x_ in (AB, MI, MT, XB, AO))
                if jj == 0:
                    after(pe, "act", ("tok", "b"))
                else:
                    after(pe, "act", ("phi", 0))
                    after(pe, "dve", ("d", 0))
                scores("ab", jj, BT_, AT_, 0)
                after(pe, "dve", ("mt1", jj))
                for g in range(2):
                    for jl, m, at in each(g):
                        ins = nc.tensor.transpose(banks[:, 2 + g, at:at + P], mt[:, g, jl, m, :], ident)
                done(ins, ("m", jj))
                scores("ak", jj, KT_, AT_, 0)
                after(pe, "act", ("m", jj))
                if jj == 0:
                    after(pe, "act", ("tok", "v"))
                for l in range(NL):
                    after(pe, "pool", ("ao", jj, l))
                    for g in range(2):
                        if l:
                            after(pe, "act", ("m", jj, l - 1, g))
                        for jl, m, at in each(g):
                            ins = mm(banks[:, 4 + g, at:at + P], ao[:, g, jl, m, :], mi[:, g, jl, m, :],
                                     start=True, stop=True)
                        done(ins, ("x", jj, l, g))
                    for g in range(2):
                        after(pe, "act", ("x", jj, l, g))
                        for jl, m, at in each(g):
                            ins = mm(banks[:, 6 + g, at:at + P], xb[:, g, jl, m, :], mt[:, g, jl, m, :],
                                     start=True, stop=True)
                        done(ins, ("mt", jj, l, g))
                    if l < NL - 1:
                        for g in range(2):
                            after(pe, "dve", ("mt", jj, l, g))
                            for jl, m, at in each(g):
                                ins = nc.tensor.transpose(banks[:, 2 + g, at:at + P], mt[:, g, jl, m, :], ident)
                            done(ins, ("m", jj, l, g))
                scores("rb", jj, BT_, RT_, 4)
                after(pe, "act", ("m", jj, NL - 2, 1))
                scores("rk", jj, KT_, RT_, 2)
                after(pe, "dve", ("ak", jj))
                a_tok, b_tok, k_tok, v_tok = (tok(x_) for x_ in (A_TOK, B_TOK, K_TOK, V_TOK))
                g2 = arena[:, G2, 0:512].rearrange("p (g j m t) -> p g j m t", g=2, j=2, m=2)
                problems = [(g, jl, m) for g in range(2) for jl in range(2) for m in range(2)]
                for q, (g, jl, m) in enumerate(problems):
                    ins = mm(banks[:, 0, q * 64:(q + 1) * 64], ab[:, g, jl, m, :], v_tok[:, 2 * jj + jl, m, rows64(g)],
                             start=True, stop=True)
                done(ins, ("g", jj))
                after(pe, "act", ("g", jj))
                after(pe, "dve", ("mt", jj, NL - 1, 1))
                for g, jl, m in problems:
                    at = (jl * 2 + m) * P
                    mm(banks[:, 6 + g, at:at + 64], mt[:, g, jl, m, :], g2[:, g, jl, m, :], start=True, stop=True)
                    ins = mm(banks[:, 6 + g, at + 64:at + P], mt[:, g, jl, m, :],
                             a_tok[:, 2 * jj + jl, m, rows64(g)], start=True, stop=True)
                done(ins, ("uw", jj))
                uw = mi
                after(pe, "act", ("uw", jj))
                after(pe, "dve", ("rk", jj))
                for g, jl, m in problems:
                    out_ = banks[rows64(g), 1, (jl * 2 + m) * P:(jl * 2 + m + 1) * P]
                    mm(out_, uw[:, g, jl, m, 0:64], xb[:, g, jl, m, :], start=True, stop=False)
                    ins = mm(out_, v_tok[:, 2 * jj + jl, m, rows64(g)], ao[:, g, jl, m, :], start=False, stop=True)
                done(ins, ("y0", jj))
                for g, jl, m in problems:
                    ins = mm(banks[rows64(g), 5, (jl * 2 + m) * P:(jl * 2 + m + 1) * P], uw[:, g, jl, m, 64:128],
                             xb[:, g, jl, m, :], start=True, stop=True)
                done(ins, ("q", jj))
                for n in (1, 2):
                    m, c = n // 2, rows64(n % 2)
                    for g in range(2):
                        for jl in range(2):
                            ins = mm(banks[rows64(g), 3 if n == 1 else 2, jl * 64:(jl + 1) * 64], uw[c, g, jl, m, 64:128],
                                     b_tok[c, 2 * jj + jl, m, rows64(g)], start=True, stop=True)
                done(ins, ("phi", jj))
                for n in range(3):
                    m, c = n // 2, rows64(n % 2)
                    for g in range(2):
                        for jl in range(2):
                            out_ = (banks[rows64(g), 7, jl * 64:(jl + 1) * 64] if n == 1 else
                                    banks[rows64(g), 4, (jl * 2 + n // 2) * 64:(jl * 2 + n // 2 + 1) * 64])
                            mm(out_, b_tok[c, 2 * jj + jl, m, rows64(g)], uw[c, g, jl, m, 0:64], start=True, stop=False)
                            ins = mm(out_, k_tok[c, 2 * jj + jl, m, rows64(g)], v_tok[c, 2 * jj + jl, m, rows64(g)],
                                     start=False, stop=True)
                done(ins, ("d", jj))
            after(pe, "act", ("phi", 1))
            after(pe, "dve", ("q", 1))
            for n in (1, 2, 3):
                if n < 3:
                    after(pe, "dve", "s1" if n == 1 else ("s", n - 1))
                    for j in range(4):
                        ins = mm(banks[:, n - 1, j * 64:(j + 1) * 64], phi[:, j, n - 1, :], state[:, j, :],
                                 start=True, stop=True)
                    done(ins, ("phi_s", n))
                after(pe, "dve", ("bd", n))
                for j in range(4):
                    ins = mm(banks[:, 2 + (n - 1) % 2, j * 64:(j + 1) * 64], state_bd[:, j, :],
                             c4(RT_)[:, j, n * CHUNK:(n + 1) * CHUNK], start=True, stop=True)
                done(ins, ("y_s", n))
                if n == 1:
                    after(pe, "dve", "y_conv_lo")
                    after(pe, "dve", ("d", 1))
                w_out_pe(pe, s, 9, (n - 1,))
            after(pe, "dve", ("y", 3))
            over_heads("mean", AT_, 0)
            after(pe, "act", "square_y")
            over_heads("var", A_TOK, 2)
            w_out_pe(pe, s, 9, (3,))
            w_out_pe(pe, s, 9, range(4, KD), lambda k: after(pe, "dve", ("y_lo", k - 4)))

        MIX = {"even": {"pe": even_pe, "act": even_act, "dve": even_dve, "pool": even_pool}}

        def big(slot, n=8 * T, m=P):
            return arena[0:m, slot:slot + 2, :].rearrange("p a b -> p (a b)")[:, 0:n]

        def heads8(slot, m=P):
            return big(slot, m=m).rearrange("p (h t) -> p h t", h=8)

        def scores4(slot):
            return big(slot, 4 * 3 * P).rearrange("p (h t) -> p h t", h=4)

        def softmax_cols(g, what):
            at = 24 * g + 8 * ("max", "shift", "sum").index(what)
            return small[:, at:at + 8].rearrange("p (h b) -> p h b", h=4)

        BLOCKS_Q = (slice(0, P), slice(P, 3 * P))

        def softmax_dve_in(dve, S, g, slot, scale):
            done = own_done(S, dve)
            wait(dve, S, "pe", ("scores", g))
            done(nc.vector.tensor_tensor(scores4(slot), banks[:, 4 * g:4 * g + 4, 0:3 * P],
                                         const("causal", P).rearrange("p (o t) -> p o t", o=1).to_broadcast([P, 4, 3 * P]),
                                         ALU.add), ("masked", g))
            for b, cols in enumerate(BLOCKS_Q):
                ins = nc.vector.reduce_max(softmax_cols(g, "max")[:, :, b:b + 1], scores4(slot)[:, :, cols], X)
            done(ins, ("max", g))
            done(nc.vector.tensor_scalar(softmax_cols(g, "shift"), softmax_cols(g, "max"), -scale, None, ALU.mult),
                 ("shift", g))

        def softmax_act(act, S, g, slot, scale):
            wait(act, S, "dve", ("shift", g))
            for h in range(4):
                for b, cols in enumerate(BLOCKS_Q):
                    ins = nc.scalar.activation(scores4(slot)[:, h, cols], scores4(slot)[:, h, cols], ACT.Exp,
                                               bias=softmax_cols(g, "shift")[:, h, b:b + 1], scale=scale,
                                               accum_out=softmax_cols(g, "sum")[:, h, b:b + 1])
            S["act"].done(ins, ("exp", g))

        def softmax_dve_out(dve, S, g, slot):
            done = own_done(S, dve)
            wait(dve, S, "act", ("exp", g))
            done(nc.vector.reciprocal(softmax_cols(g, "max"), softmax_cols(g, "sum")), ("recip", g))
            for b, cols in enumerate(BLOCKS_Q):
                v = scores4(slot)[:, :, cols]
                ins = nc.vector.tensor_tensor(v, v, softmax_cols(g, "max")[:, :, b:b + 1].to_broadcast(
                    [P, 4, cols.stop - cols.start]), ALU.mult)
            done(ins, ("probs", g))

        def probs_transposed_pe(pe, S, g, slot):
            wait(pe, S, "dve", ("probs", g))
            for h in range(4):
                for c in range(3):
                    ins = nc.tensor.transpose(banks[:, 4 * g + h, c * P:(c + 1) * P],
                                              scores4(slot)[:, h, c * P:(c + 1) * P], ident)
            S["pe"].done(ins, ("probsT", g))

        def probs_transposed_act(act, S, g, slot):
            wait(act, S, "pe", ("probsT", g))
            S["act"].done(nc.scalar.copy(scores4(slot), banks[:, 4 * g:4 * g + 4, 0:3 * P]), ("probsT", g))

        def own_done(S, eng):
            def done(ins, name):
                S["dve"].done(ins, name)
                eng.wait_ge(S["dve"].sem, S["dve"].finished)
            return done

        def wait(eng, S, who, name):
            eng.wait_ge(S[who].sem, S[who].value[name])

        def sum_of(pe, pieces, out):
            for i, piece in enumerate(pieces):
                m = piece.shape[0]
                ins = nc.tensor.matmul(out, const("ones", m), piece, start=i == 0, stop=i == len(pieces) - 1)
            return ins

        def stage_steps(kind, names):
            if kind not in stages:
                return {}
            return {eng: Steps(sem(f"{kind}_{eng}_steps"), n) for eng, n in names.items()}

        M_CQ, M_CKV, M_SQ, M_Q32, M_KV32, M_SQ2, M_QN, M_QR, M_KN, M_KR, M_V, M_BIG, M_RSQ, M_RSK, M_RS = \
            0, 1, 2, 3, 4, 5, 6, 8, 10, 12, 14, 16, 18, 2, 20
        M_S, M_PT = (16, 18), (0, 2)
        MS = stage_steps("mla", {
            "pe": [("tile", 0), ("tile", 3), "ss_cq", "ss_ckv"] + [("q", i) for i in range(3)]
                  + [("k", i) for i in range(3)] + ["v"] + [("r", i) for i in range(3)] + ["ss_q", "ss_k", "rot_q", "rot_k"]
                  + [("scores", 0), ("scores", 1), ("probsT", 0), ("probsT", 1), ("o", 0), ("o", 1)],
            "act": ["sin", "cos"] + [("evac", i) for i in range(6)] + ["sq_c", "ln_c", "rs_c", "hi_c"]
                   + [("q", i) for i in range(4)] + [("k", i) for i in range(4)] + ["v"] + [("r", i) for i in range(4)]
                   + ["sq_q", "sq_qr", "ln_q", "rs_q", "sq_k", "ln_k", "rs_k"]
                   + [("exp", 0), ("exp", 1), ("probsT", 0), ("probsT", 1), ("hi", 0), ("hi", 1)],
            "dve": ["pos", "ang", "turn", "round", "red0", "red1", "red2", "clamp", "abs", "cosarg"]
                   + ["c32", "c_lo", "q_n", "q_r", "qsin", "qcos", "q_rope", "kpe_g", "kpe_sin", "kpe_cos", "kpe_rope",
                      "k_n", "k_r"]
                   + [(n, g) for g in range(2) for n in ("masked", "max", "shift")]
                   + [(n, g) for g in range(2) for n in ("recip", "probs")] + [("lo", 0), ("lo", 1)]})
        cq = arena[:, M_CQ, 0:768].rearrange("p (j t) -> p j t", j=3)
        ckv = arena[:, M_CKV, 0:512].rearrange("p (j t) -> p j t", j=2)
        kpe = arena[0:64, M_CKV, 512:768]
        kpe_g = arena[0:64, M_CKV, 768:1024]
        cos, sin = arena[0:64, M_KV32, 512:768], arena[0:64, M_KV32, 768:1024]
        ang, turn = arena[0:64, M_V, 0:T], arena[0:64, M_V, T:2 * T]
        red, pos = arena[0:64, M_V, 2 * T:3 * T], arena[0:64, M_V + 1, 0:T].bitcast(I32)
        v_mla = big(M_V).rearrange("p (b c) -> p b c", b=2)

        ENDS = {("tile", 1): (0, 0), ("tile", 2): (0, 1), ("tile", 4): (1, 0), ("tile", 5): (1, 1),
                ("q", 3): (2, 1), ("k", 3): (3, 0), ("r", 3): (4, 1)}

        def tile_there(eng, s, name):
            if name in ENDS:
                part_used(eng, s, *ENDS[name])
            else:
                wait(eng, MS, "pe", name)

        def over8(ap):
            return ap.rearrange("p (o t) -> p o t", o=1).to_broadcast([64, 8, T])

        positions_loaded = sem("positions_loaded")

        def mla_pool(pool, s):
            if s:
                pool.wait_ge(x_ready, 4 * s)
            pool.dma_start(pos, positions.to_broadcast([64, T])).then_inc(positions_loaded, 16)

        def mla_act(act, s):
            done = MS["act"].done
            cp = nc.scalar.copy
            hi_gu(act, *unit(s, 0))
            norm_act(act, s)
            split_act(act, s, 0)
            wait(act, MS, "dve", "cosarg")
            done(nc.scalar.activation(sin, red, ACT.Sin), "sin")
            done(nc.scalar.activation(cos, turn, ACT.Sin), "cos")

            def evac(i):
                tile_there(act, s, ("tile", i))
                dst = cq[:, i, :] if i < 3 else ckv[:, i - 3, :] if i < 5 else kpe
                done(cp(dst, banks[0:dst.shape[0], i % 4, 0:T]), ("evac", i))

            for i in range(3):
                evac(i)
            split_act(act, s, 1)
            for i in range(3, 6):
                evac(i)
            wait(act, MS, "act", ("evac", 5))
            nc.scalar.activation(flat(M_SQ, 768), flat(M_CQ, 768), ACT.Square)
            nc.scalar.activation(flat(M_SQ2, 512), flat(M_CKV, 512), ACT.Square)
            done(nc.scalar.activation(arena[0:64, M_SQ2, 512:768], kpe, ACT.Square), "sq_c")
            split_act(act, s, 2)
            wait(act, MS, "pe", "ss_ckv")
            rs = arena[:, M_RS, 0:512].rearrange("p (b t) -> p b t", b=2)
            for i, width in enumerate((Q_RANK, KV_RANK)):
                ins = nc.scalar.activation(rs[:, i, :], banks[:, 6 + i, 0:T], ACT.Ln, scale=1.0 / width, bias=eps_col[:, 0:1])
            done(ins, "ln_c")
            wait(act, MS, "act", "ln_c")
            done(nc.scalar.activation(rs, rs, ACT.Exp, scale=-0.5), "rs_c")
            wait(act, MS, "dve", "c32")
            cp(h_hi[:, 0:3, :], flat(M_Q32, 768).rearrange("p (j t) -> p j t", j=3))
            done(cp(h_hi[:, 3:5, :], flat(M_KV32, 512).rearrange("p (j t) -> p j t", j=2)), "hi_c")

            def evac2(name, i, slot, m=P):
                tile_there(act, s, (name, i))
                done(cp(big(slot, m=m)[:, i * 512:(i + 1) * 512], banks[0:m, i, :]), (name, i))

            for i in range(4):
                evac2("q", i, M_QN)
            split_act(act, s, 3)
            for i in range(4):
                evac2("k", i, M_KN)
            split_act(act, s, 4)
            wait(act, MS, "pe", "v")
            done(cp(big(M_V).rearrange("p (b n) -> p b n", b=4), banks[:, 4:8, :]), "v")
            for i in range(4):
                evac2("r", i, M_QR, 64)
            split_act(act, s, 5)
            wait(act, MS, "act", ("r", 3))
            done(nc.scalar.activation(big(M_BIG), big(M_QN), ACT.Square), "sq_q")
            done(nc.scalar.activation(big(M_KR, m=64), big(M_QR, m=64), ACT.Square), "sq_qr")
            wait(act, MS, "pe", "ss_q")
            four = lambda slot: big(slot).rearrange("p (b n) -> p b n", b=4)
            done(nc.scalar.activation(four(M_RSQ), banks[:, 0:4, :], ACT.Ln, scale=1.0 / QK_DIM, bias=eps_col[:, 0:1]), "ln_q")
            wait(act, MS, "act", "ln_q")
            done(nc.scalar.activation(big(M_RSQ), big(M_RSQ), ACT.Exp, scale=-0.5), "rs_q")
            done(nc.scalar.activation(big(M_BIG), big(M_KN), ACT.Square), "sq_k")
            wait(act, MS, "pe", "ss_k")
            wait(act, MS, "dve", "c_lo")
            done(nc.scalar.activation(four(M_RSK), banks[:, 4:8, :], ACT.Ln, scale=1.0 / QK_DIM, bias=eps_col[:, 0:1]), "ln_k")
            wait(act, MS, "act", "ln_k")
            done(nc.scalar.activation(big(M_RSK), big(M_RSK), ACT.Exp, scale=-0.5), "rs_k")
            for g in range(2):
                softmax_act(act, MS, g, M_S[g], MLA_SCALE)
            for g in range(2):
                probs_transposed_act(act, MS, g, M_PT[g])
            for g in range(2):
                wait(act, MS, "pe", ("o", g))
                done(cp(h_hi[:, 4 * g:4 * g + 4, :].rearrange("p (b i) t -> p b (i t)", b=2), banks[:, 4 * g:4 * g + 2, :]),
                     ("hi", g))
            split_act(act, s, 6)
            hi_dn(act, *unit(s, 7), 64)

        def mla_dve(dve, s):
            done = own_done(MS, dve)
            tt, ts, stt = nc.vector.tensor_tensor, nc.vector.tensor_scalar, nc.vector.scalar_tensor_tensor
            first_lo_gu(dve, s)
            norm_dve(dve, s)
            dve.wait_ge(positions_loaded, 16)
            done(nc.vector.tensor_copy(ang, pos), "pos")
            done(ts(ang, ang, const("inv_freq", 64), None, ALU.mult), "ang")
            done(ts(turn, ang, float(1 / (2 * np.pi)), None, ALU.mult), "turn")
            done(ts(turn, turn, 1.5 * 2.0 ** 23, 1.5 * 2.0 ** 23, ALU.add, ALU.subtract), "round")
            for i, part in enumerate(TWO_PI):
                done(stt(out=red, in0=turn, scalar=-part, in1=ang if i == 0 else red, op0=ALU.mult, op1=ALU.add), f"red{i}")
            done(ts(red, red, 3.1415925, -3.1415925, ALU.min, ALU.max), "clamp")
            done(stt(out=turn, in0=red, scalar=-1.0, in1=red, op0=ALU.mult, op1=ALU.max), "abs")
            done(ts(turn, turn, -1.0, float(np.pi / 2), ALU.mult, ALU.add), "cosarg")
            split_dve(dve, s, 0)
            split_dve(dve, s, 1)
            split_dve(dve, s, 2)
            wait(dve, MS, "act", "rs_c")
            rs = arena[:, M_RS, 0:512].rearrange("p (b t) -> p b t", b=2)
            q32 = flat(M_Q32, 768).rearrange("p (j t) -> p j t", j=3)
            kv32 = flat(M_KV32, 512).rearrange("p (j t) -> p j t", j=2)
            for j in range(3):
                stt(out=q32[:, j, :], in0=cq[:, j, :], scalar=pcol("q_a", j), in1=rs[:, 0, :], op0=ALU.mult, op1=ALU.mult)
            for j in range(2):
                ins = stt(out=kv32[:, j, :], in0=ckv[:, j, :], scalar=pcol("kv_a", j), in1=rs[:, 1, :],
                          op0=ALU.mult, op1=ALU.mult)
            done(ins, "c32")
            wait(dve, MS, "act", "hi_c")
            tt(h_lo[:, 0:3, :], q32, h_hi[:, 0:3, :].bitcast(F32), ALU.subtract)
            done(tt(h_lo[:, 3:5, :], kv32, h_hi[:, 3:5, :].bitcast(F32), ALU.subtract), "c_lo")
            split_dve(dve, s, 3)
            split_dve(dve, s, 4)
            split_dve(dve, s, 5)
            wait(dve, MS, "act", "rs_q")
            done(stt(out=big(M_QN), in0=big(M_QN), scalar=pcol("q_nope"), in1=big(M_RSQ), op0=ALU.mult, op1=ALU.mult), "q_n")
            done(stt(out=big(M_QR, m=64), in0=big(M_QR, m=64), scalar=pcol("q_rope", 0, 64), in1=big(M_RSQ, m=64),
                     op0=ALU.mult, op1=ALU.mult), "q_r")
            wait(dve, MS, "pe", "rot_q")
            done(tt(heads8(M_BIG, 64).rearrange("p (b i) t -> p b i t", b=4),
                    banks[0:64, 0:4, :].rearrange("p b (i t) -> p b i t", i=2),
                    sin.rearrange("p (o q t) -> p o q t", o=1, q=1).to_broadcast([64, 4, 2, T]), ALU.mult), "qsin")
            done(tt(heads8(M_QR, 64), heads8(M_QR, 64), over8(cos), ALU.mult), "qcos")
            done(tt(big(M_QR, m=64), big(M_QR, m=64), big(M_BIG, m=64), ALU.add), "q_rope")
            done(ts(kpe_g, kpe, pcol("k_rope", 0, 64), None, ALU.mult), "kpe_g")
            wait(dve, MS, "pe", "rot_k")
            done(tt(kpe, banks[0:64, 4, 0:T], sin, ALU.mult), "kpe_sin")
            done(tt(kpe_g, kpe_g, cos, ALU.mult), "kpe_cos")
            done(tt(kpe_g, kpe_g, kpe, ALU.add), "kpe_rope")
            wait(dve, MS, "act", "rs_k")
            done(stt(out=big(M_KN), in0=big(M_KN), scalar=pcol("k_nope"), in1=big(M_RSK), op0=ALU.mult, op1=ALU.mult), "k_n")
            done(tt(heads8(M_KR, 64), over8(kpe_g), heads8(M_RSK, 64), ALU.mult), "k_r")
            for g in range(2):
                softmax_dve_in(dve, MS, g, M_S[g], MLA_SCALE)
            for g in range(2):
                softmax_dve_out(dve, MS, g, M_S[g])
            for g in range(2):
                wait(dve, MS, "act", ("hi", g))
                y = slice(4 * g, 4 * g + 4)
                done(tt(h_lo[:, y, :].rearrange("p (b i) t -> p b (i t)", b=2), banks[:, 4 * g:4 * g + 2, :],
                        h_hi[:, y, :].rearrange("p (b i) t -> p b (i t)", b=2).bitcast(F32), ALU.subtract), ("lo", g))
            split_dve(dve, s, 6)
            lo_dn(dve, *unit(s, 7), 64)
            add_to_x(dve, s)

        def mla_pe(pe, s):
            done = MS["pe"].done
            mm = nc.tensor.matmul
            norm_pe(pe, s)

            w = gu_weights(pe, s, 0)
            done(channel_tile(banks[:, 0, 0:T], w, 0, norm=s), ("tile", 0))
            channel_tile(banks[:, 1, 0:T], w, DN).then_inc(gu_used, 1)
            channel_tile(banks[:, 2, 0:T], dn_weights(pe, s, 0), 0).then_inc(dn_used, 1)
            w = gu_weights(pe, s, 1)
            done(channel_tile(banks[:, 3, 0:T], w, 0), ("tile", 3))
            wait(pe, MS, "act", ("evac", 0))
            channel_tile(banks[:, 0, 0:T], w, DN).then_inc(gu_used, 1)
            wait(pe, MS, "act", ("evac", 1))
            channel_tile(banks[0:64, 1, 0:T], dn_weights(pe, s, 1), 0, 64).then_inc(dn_used, 1)
            wait(pe, MS, "act", "sq_c")
            done(sum_of(pe, [arena[:, M_SQ, i * T:(i + 1) * T] for i in range(3)], banks[:, 6, 0:T]), "ss_cq")
            done(sum_of(pe, [arena[:, M_SQ2, i * T:(i + 1) * T] for i in range(2)], banks[:, 7, 0:T]), "ss_ckv")
            wait(pe, MS, "dve", "c_lo")

            def h_block(k, cols=slice(0, T)):
                return h_hi[:, k, cols], h_lo[:, k, cols]

            gu, dn = gu_weights(pe, s, 2), dn_weights(pe, s, 2)
            for h in range(HEADS):
                for k in range(3):
                    b = 3 * h + k
                    w = gu(b * P, P) if b < GU // P else dn(b * P - GU, P)
                    ins = three_products(banks[:, h // 2, h % 2 * T:(h % 2 + 1) * T], w, h_block(k), k == 0, k == 2)
                    if b == GU // P - 1:
                        ins.then_inc(gu_used, 1)
                if h == HEADS - 1:
                    ins.then_inc(dn_used, 1)
                elif h % 2:
                    done(ins, ("q", h // 2))
            gu = gu_weights(pe, s, 3)
            for h in range(HEADS):
                if h % 2 == 0:
                    wait(pe, MS, "act", ("q", h // 2))
                for k in range(2):
                    ins = three_products(banks[:, h // 2, h % 2 * T:(h % 2 + 1) * T], gu((2 * h + k) * P, P),
                                         h_block(3 + k), k == 0, k == 1)
                if h == HEADS - 1:
                    ins.then_inc(gu_used, 1)
                elif h % 2:
                    done(ins, ("k", h // 2))
            wait(pe, MS, "act", "ln_c")
            for k in range(2):
                w = (dn_weights, gu_weights)[k](pe, s, 3 + k)
                for t in range(2):
                    for c in range(2):
                        ins = three_products(banks[:, 4 + 2 * t + c, :], h_block(3 + k, slice(t * P, (t + 1) * P)),
                                             w(c * 512, 512), k == 0, k == 1)
                if k == 0:
                    ins.then_inc(dn_used, 1)
            done(ins, "v")
            gu, dn = gu_weights(pe, s, 4), dn_weights(pe, s, 4)
            for h in range(HEADS):
                if h % 2 == 0:
                    wait(pe, MS, "act", ("k", h // 2))
                for k in range(3):
                    b = 3 * h + k
                    w = gu(D + b * 64, 64) if b < 16 else dn((b - 16) * 64, 64)
                    ins = three_products(banks[0:64, h // 2, h % 2 * T:(h % 2 + 1) * T], w, h_block(k), k == 0, k == 2)
                    if b == 15:
                        ins.then_inc(gu_used, 1)
                if h == HEADS - 1:
                    ins.then_inc(dn_used, 1)
                elif h % 2:
                    done(ins, ("r", h // 2))

            wait(pe, MS, "act", "sq_qr")
            for i in range(4):
                ins = sum_of(pe, [big(M_BIG)[:, i * 512:(i + 1) * 512], big(M_KR, m=64)[:, i * 512:(i + 1) * 512]],
                             banks[:, i, :])
            done(ins, "ss_q")
            wait(pe, MS, "act", "sq_k")
            wait(pe, MS, "act", "v")
            pe_sq = arena[0:64, M_SQ2, 512:768]
            for i in range(4):
                mm(banks[:, 4 + i, :], const("ones"), big(M_BIG)[:, i * 512:(i + 1) * 512], start=True, stop=False)
                for j in range(2):
                    ins = mm(banks[:, 4 + i, j * T:(j + 1) * T], const("ones", 64), pe_sq, start=False, stop=j == 1)
            done(ins, "ss_k")
            wait(pe, MS, "dve", "q_r")
            for i in range(4):
                ins = mm(banks[0:64, i, :], const("rot", 64), big(M_QR, m=64)[:, i * 512:(i + 1) * 512], start=True, stop=True)
            done(ins, "rot_q")
            wait(pe, MS, "dve", "kpe_g")
            wait(pe, MS, "act", "ln_k")
            done(mm(banks[0:64, 4, 0:T], const("rot", 64), kpe_g, start=True, stop=True), "rot_k")
            wait(pe, MS, "dve", "k_r")
            for g in range(2):
                for hh in range(4):
                    h = 4 * g + hh
                    for q, keys, cols in ((0, slice(0, P), BLOCKS_Q[0]), (1, slice(0, T), BLOCKS_Q[1])):
                        tok_q = slice(q * P, (q + 1) * P)
                        mm(banks[:, h, cols], heads8(M_QN)[:, h, tok_q], heads8(M_KN)[:, h, keys], start=True, stop=False)
                        ins = mm(banks[:, h, cols], heads8(M_QR, 64)[:, h, tok_q], heads8(M_KR, 64)[:, h, keys],
                                 start=False, stop=True)
                done(ins, ("scores", g))
            for g in range(2):
                probs_transposed_pe(pe, MS, g, M_S[g])
            for g in range(2):
                wait(pe, MS, "act", ("probsT", g))
                for hh in range(4):
                    h = 4 * g + hh
                    o = banks[:, 4 * g + hh // 2, hh % 2 * T:(hh % 2 + 1) * T]
                    pt = scores4(M_PT[g])[:, hh, :]
                    mm(o, v_mla[:, 0, h * P:(h + 1) * P], pt[:, 0:T], start=True, stop=False)
                    ins = mm(o[:, P:T], v_mla[:, 1, h * P:(h + 1) * P], pt[:, T:3 * P], start=False, stop=True)
                done(ins, ("o", g))

            def ready(k):
                if k == 0:
                    wait(pe, MS, "dve", ("lo", 1))
            w_out_pe(pe, s, 5, range(KD), ready)

        MIX["mla"] = {"pe": mla_pe, "act": mla_act, "dve": mla_dve, "pool": mla_pool}

        F_A, F_G, F_Q, F_K, F_V, F_U, F_ACC, F_CUM, F_Y, F_SQ, F_RS = 0, 1, 2, 3, 4, 5, 7, 8, 17, 18, 19
        F_S, F_PT = (9, 11), (13, 15)
        TAPS_DURING = 3
        TAPS = (4 * TAPS_DURING, 18, 24, 26, LONG_TAPS)
        FX = stage_steps("fox", {
            "pe": [("tile", i) for i in range(0, 16, 3)] + [("scores", 0), ("scores", 1)]
                  + [("probsT", 0), ("probsT", 1), ("o", 0), ("o", 1), "ss_attn", "mean", "var", "ss_conv"],
            "act": [("evac", i) for i in range(16)] + ["v", "exp_f", "ln_f", ("exp", 0), ("exp", 1),
                   ("probsT", 0), ("probsT", 1), ("o", 0), ("o", 1), "sq_attn", "ln_attn", "rs_attn", "hi_attn",
                   "sq_var", "ln_var", "rs_var", "silu", "sq_conv", "ln_conv", "rs_conv"]
                   + [("hi_conv", j) for j in range(4)],
            "dve": ["u"] + [("tap", 0)] + [("tap", i) for i in range(1, 4 * TAPS_DURING)] + ["z", "nabs", "min0", "logf", "cum", "neg"]
                   + [n for g in range(2) for n in [("tap", i) for i in range(TAPS[g], TAPS[g + 1])]
                      + [("masked", g), ("max", g), ("shift", g)]]
                   + [("tap", i) for i in range(TAPS[2], TAPS[3])]
                   + [(n, g) for g in range(2) for n in ("recip", "probs")]
                   + [("tap", i) for i in range(TAPS[3], LONG_TAPS)] + ["attn", "lo_attn"] + ["centred", "normed", "affine"]
                   + [n for j in range(5) for n in [("conv", j)] * (j < 4) + [("lo_conv", j - 1)] * (j > 0)],
            "pool": ["pads", "ones"]})
        u_pad = arena[:, F_U:F_U + 2, :].rearrange("p a b -> p (a b)")[:, 0:4 * (T + PAD)].rearrange(
            "p (j t) -> p j t", j=4)
        v_fox = flat(F_V).rearrange("p (b c) -> p b c", b=2)
        FR = 72
        f_z, f_cum, f_neg, f_one = (arena[0:FR, F_CUM, i * T:(i + 1) * T] for i in range(4))
        f_abs = arena[0:FR, F_SQ, 0:T]

        def fox_pool(pool, s):
            if s:
                pool.wait_ge(x_ready, 4 * s)
            done = FX["pool"].done
            done(nc.gpsimd.memset(u_pad[:, :, 0:PAD], 0.0), "pads")
            done(nc.gpsimd.memset(f_one, 1.0), "ones")

        def rstd_steps(act, S, name, src, dst, width):
            S["act"].done(nc.scalar.activation(dst, src, ACT.Ln, scale=1.0 / width, bias=eps_col[:, 0:1]), "ln_" + name)
            wait(act, S, "act", "ln_" + name)
            S["act"].done(nc.scalar.activation(dst, dst, ACT.Exp, scale=-0.5), "rs_" + name)

        def fox_act(act, s):
            done = FX["act"].done
            cp = nc.scalar.copy
            hi_gu(act, *unit(s, 0))
            norm_act(act, s)

            def evac(i):
                if i % 3:
                    part_used(act, s, i // 3, i % 3 - 1)
                else:
                    wait(act, FX, "pe", ("tile", i))
                src, dst = banks[:, i % 4, 0:T], c4((F_A, F_G, F_Q, F_K)[i // 4])[:, i % 4, :]
                func, scale = {1: (ACT.Sigmoid, 1.0), 2: (ACT.Copy, FOX_SCALE)}.get(i // 4, (ACT.Copy, 1.0))
                done(nc.scalar.activation(dst, src, func, scale=scale), ("evac", i))

            for u in range(5):
                split_act(act, s, u)
                for i in range(3 * u, 3 * u + 3):
                    evac(i)
            split_act(act, s, 5)
            evac(15)
            split_act(act, s, 6, 8 * FR)
            part_used(act, s, 6, 0)
            done(cp(v_fox, banks[:, 4:6, :]), "v")
            wait(act, FX, "dve", "nabs")
            done(nc.scalar.activation(f_abs, f_abs, ACT.Exp), "exp_f")
            wait(act, FX, "act", "exp_f")
            wait(act, FX, "pool", "ones")
            done(nc.scalar.activation(f_abs, f_abs, ACT.Ln, bias=f_one[:, 0:1]), "ln_f")
            split_act(act, s, 7)
            for g in range(2):
                softmax_act(act, FX, g, F_S[g], 1.0)
            for g in range(2):
                probs_transposed_act(act, FX, g, F_PT[g])
            for g in range(2):
                wait(act, FX, "pe", ("o", g))
                done(cp(flat(F_Y)[:, g * 512:(g + 1) * 512], banks[:, 4 * g, :]), ("o", g))
            wait(act, FX, "act", ("o", 1))
            done(nc.scalar.activation(flat(F_SQ), flat(F_Y), ACT.Square), "sq_attn")
            wait(act, FX, "pe", "ss_attn")
            rs = [arena[:, F_RS, i * T:(i + 1) * T] for i in range(3)]
            rstd_steps(act, FX, "attn", banks[:, 1, 0:T], rs[0], RW)
            wait(act, FX, "dve", "attn")
            done(cp(h_hi[:, 4:8, :], c4(F_Y)), "hi_attn")
            split_act(act, s, 8)
            hi_dn(act, *unit(s, 9), 64)
            wait(act, FX, "dve", "centred")
            done(nc.scalar.activation(flat(F_SQ), flat(F_ACC), ACT.Square), "sq_var")
            wait(act, FX, "pe", "var")
            rstd_steps(act, FX, "var", banks[:, 3, 0:T], rs[1], RW)
            wait(act, FX, "dve", "affine")
            done(nc.scalar.activation(flat(F_ACC), flat(F_ACC), ACT.Silu), "silu")
            wait(act, FX, "act", "silu")
            done(nc.scalar.activation(flat(F_SQ), flat(F_ACC), ACT.Square), "sq_conv")
            wait(act, FX, "pe", "ss_conv")
            rstd_steps(act, FX, "conv", banks[:, 0, 0:T], rs[2], RW)
            for j in range(4):
                wait(act, FX, "dve", ("conv", j))
                done(cp(h_hi[:, j, :], c4(F_ACC)[:, j, :]), ("hi_conv", j))

        def fox_dve(dve, s):
            done = own_done(FX, dve)
            tt, ts, stt = nc.vector.tensor_tensor, nc.vector.tensor_scalar, nc.vector.scalar_tensor_tensor
            first_lo_gu(dve, s)
            norm_dve(dve, s)
            acc = c4(F_ACC)

            def taps(first, last):
                for tap in range(first, last):
                    for j in range(4):
                        w, src = pcol("long_w", 4 * tap + j), u_pad[:, j, tap:tap + T]
                        if tap == 0:
                            ins = ts(acc[:, j, :], src, w, pcol("long_b", j), ALU.mult, ALU.add)
                        else:
                            ins = stt(out=acc[:, j, :], in0=src, scalar=w, in1=acc[:, j, :], op0=ALU.mult, op1=ALU.add)
                    done(ins, ("tap", tap))

            for u in range(3):
                split_dve(dve, s, u)
            wait(dve, FX, "act", ("evac", 7))
            wait(dve, FX, "pool", "ones")
            done(tt(u_pad[:, :, PAD:PAD + T], c4(F_A), c4(F_G), ALU.mult), "u")
            for i, u in enumerate((3, 4, 5, 6)):
                split_dve(dve, s, u, 8 * FR if u == 6 else DN)
                taps(TAPS_DURING * i, TAPS_DURING * (i + 1))
            part_used(dve, s, 6, 1)
            done(ts(f_z, banks[0:FR, 6, 0:T], pcol("forget_b", 0, FR), None, ALU.add), "z")
            done(stt(out=f_abs, in0=f_z, scalar=-1.0, in1=f_z, op0=ALU.mult, op1=ALU.min), "nabs")
            done(ts(f_z, f_z, 0.0, None, ALU.min), "min0")
            wait(dve, FX, "act", "ln_f")
            done(tt(f_z, f_z, f_abs, ALU.subtract), "logf")
            done(nc.vector.tensor_tensor_scan(f_cum, f_one, f_z, 0.0, ALU.mult, ALU.add), "cum")
            done(ts(f_neg, f_cum, -1.0, None, ALU.mult), "neg")
            split_dve(dve, s, 7)
            for g in range(2):
                taps(TAPS[g], TAPS[g + 1])
                softmax_dve_in(dve, FX, g, F_S[g], 1.0)
            taps(TAPS[2], TAPS[3])
            for g in range(2):
                softmax_dve_out(dve, FX, g, F_S[g])
            taps(TAPS[3], LONG_TAPS)
            rs = [arena[:, F_RS, i * T:(i + 1) * T] for i in range(3)]
            wait(dve, FX, "act", "rs_attn")
            for j in range(4):
                ins = stt(out=c4(F_Y)[:, j, :], in0=c4(F_Y)[:, j, :], scalar=pcol("out_attn", j), in1=rs[0],
                          op0=ALU.mult, op1=ALU.mult)
            done(ins, "attn")
            wait(dve, FX, "act", "hi_attn")
            done(tt(h_lo[:, 4:8, :], c4(F_Y), h_hi[:, 4:8, :].bitcast(F32), ALU.subtract), "lo_attn")
            over4 = lambda ap: ap.rearrange("p (o t) -> p o t", o=1).to_broadcast([P, 4, T])
            wait(dve, FX, "pe", "mean")
            done(stt(out=acc, in0=over4(banks[:, 2, 0:T]), scalar=-1.0 / RW, in1=acc, op0=ALU.mult, op1=ALU.add), "centred")
            split_dve(dve, s, 8)
            lo_dn(dve, *unit(s, 9), 64)
            wait(dve, FX, "act", "rs_var")
            done(tt(acc, acc, over4(rs[1]), ALU.mult), "normed")
            for j in range(4):
                ins = ts(acc[:, j, :], acc[:, j, :], pcol("cln_g", j), pcol("cln_b", j), ALU.mult, ALU.add)
            done(ins, "affine")
            wait(dve, FX, "act", "rs_conv")
            for j in range(5):
                if j < 4:
                    done(stt(out=acc[:, j, :], in0=acc[:, j, :], scalar=pcol("out_conv", j), in1=rs[2],
                             op0=ALU.mult, op1=ALU.mult), ("conv", j))
                if j > 0:
                    wait(dve, FX, "act", ("hi_conv", j - 1))
                    done(tt(h_lo[:, j - 1, :], acc[:, j - 1, :], h_hi[:, j - 1, :].bitcast(F32), ALU.subtract),
                         ("lo_conv", j - 1))
            add_to_x(dve, s)

        def fox_pe(pe, s):
            done = FX["pe"].done
            mm = nc.tensor.matmul
            norm_pe(pe, s)

            def tile(i, w, base):
                if i >= 4:
                    wait(pe, FX, "act", ("evac", i - 4))
                return channel_tile(banks[:, i % 4, 0:T], w, base, norm=s if i == 0 else None)

            for u in range(5):
                w = gu_weights(pe, s, u)
                done(tile(3 * u, w, 0), ("tile", 3 * u))
                tile(3 * u + 1, w, DN).then_inc(gu_used, 1)
                tile(3 * u + 2, dn_weights(pe, s, u), 0).then_inc(dn_used, 1)

            def values(w, k, base):
                for t in range(2):
                    ins = three_products(banks[:, 4 + t, :], (h_hi[:, k, t * P:(t + 1) * P], h_lo[:, k, t * P:(t + 1) * P]),
                                         w(base, RW), k == 0, k == KD - 1)
                return ins

            w = gu_weights(pe, s, 5)
            done(tile(15, w, 0), ("tile", 15))
            values(w, 0, DN)
            values(w, 1, DN + RW).then_inc(gu_used, 1)
            w = dn_weights(pe, s, 5)
            values(w, 2, 0)
            values(w, 3, RW).then_inc(dn_used, 1)
            w = gu_weights(pe, s, 6)
            for k in range(4, KD):
                ins = values(w, k, (k - 4) * RW)
            ins.then_inc(gu_used, 1)
            channel_tile(banks[0:FR, 6, 0:T], dn_weights(pe, s, 6), 0, FR).then_inc(dn_used, 1)
            wait(pe, FX, "act", ("evac", 15))
            wait(pe, FX, "dve", "neg")
            for g in range(2):
                if g:
                    wait(pe, FX, "act", "v")
                for hh in range(4):
                    h = 4 * g + hh
                    r, j = rows64(h % 2), h // 2
                    r8 = slice(64 * (h % 2), 64 * (h % 2) + 8)
                    one = ident[r8, r8.start + h:r8.start + h + 1]
                    for q, n, cols in ((0, P, BLOCKS_Q[0]), (1, T, BLOCKS_Q[1])):
                        tq = slice(q * P, (q + 1) * P)
                        out_ = banks[:, h, cols]
                        mm(out_, c4(F_Q)[r, j, tq], c4(F_K)[r, j, 0:n], start=True, stop=False)
                        mm(out_, arena[r8, F_CUM, T + q * P:T + (q + 1) * P], one.to_broadcast([8, n]), start=False, stop=False)
                        ins = mm(out_, one.to_broadcast([8, P]), arena[r8, F_CUM, 2 * T:2 * T + n], start=False, stop=True)
                done(ins, ("scores", g))
            for g in range(2):
                probs_transposed_pe(pe, FX, g, F_S[g])
            for g in range(2):
                wait(pe, FX, "act", ("probsT", g))
                for hh in range(4):
                    h = 4 * g + hh
                    o = banks[rows64(h % 2), 4 * g, hh // 2 * T:(hh // 2 + 1) * T]
                    pt = scores4(F_PT[g])[:, hh, :]
                    mm(o, v_fox[:, 0, h * 64:(h + 1) * 64], pt[:, 0:T], start=True, stop=False)
                    ins = mm(o[:, P:T], v_fox[:, 1, h * 64:(h + 1) * 64], pt[:, T:3 * P], start=False, stop=True)
                done(ins, ("o", g))
            blocks4 = lambda slot: [c4(slot)[:, j, :] for j in range(4)]
            wait(pe, FX, "act", "sq_attn")
            done(sum_of(pe, blocks4(F_SQ), banks[:, 1, 0:T]), "ss_attn")
            wait(pe, FX, "dve", ("tap", LONG_TAPS - 1))
            done(sum_of(pe, blocks4(F_ACC), banks[:, 2, 0:T]), "mean")
            wait(pe, FX, "dve", "lo_attn")
            w_out_pe(pe, s, 7, range(3), turn=4)
            wait(pe, FX, "act", "sq_var")
            done(sum_of(pe, blocks4(F_SQ), banks[:, 3, 0:T]), "var")
            w_out_pe(pe, s, 7, (3,), turn=4)
            wait(pe, FX, "act", "sq_conv")
            done(sum_of(pe, blocks4(F_SQ), banks[:, 0, 0:T]), "ss_conv")

            w_out_pe(pe, s, 7, range(4, KD), lambda k: wait(pe, FX, "dve", ("lo_conv", k - 4)), turn=4)

        MIX["fox"] = {"pe": fox_pe, "act": fox_act, "dve": fox_dve, "pool": fox_pool}

        block = ctx.enter_context(nc.Block())

        @block.sync
        def _(sp):
            for t in range(2):
                sp.dma_start(x[:, t, :], x_in[:, t, :]).then_inc(x_loaded[t], 16)

            def load(pair, p):
                count(sp, gu_lo_ready, 2 * pair + p - 1)
                sp.dma_start(raw_gu[:, p, :], units_gu[bass.ds(2 * pair + p, 1), :, :].rearrange("a p n -> p (a n)")
                             ).then_inc(gu_landed[p], 16)
                count(sp, dn_lo_ready, 2 * pair + p - 1)
                sp.dma_start(raw_dn[:, p, :], units_dn[bass.ds(2 * pair + p, 1), :, :].rearrange("a p n -> p (a n)")
                             ).then_inc(dn_landed[p], 16)

            load(0, 0)
            load(0, 1)
            rest = slice(CONST_COLS["ones"].stop, CONSTS)
            sp.dma_start(cst[:, rest], constants[:, rest]).then_inc(consts_loaded, 16)
            sp.dma_start(lora[:, :, :], low_rank).then_inc(consts_loaded, 16)
            with sp.Fori(1, n_units // 2) as pair:
                load(pair, 0)
                load(pair, 1)
            sp.wait_ge(x_ready, 4 * len(stages) - 4)
            sp.dma_start(gain_row, final_gain.to_broadcast([P, D])).then_inc(gain_loaded, 16)
            sp.wait_ge(x_ready, 4 * len(stages) + 2)
            sp.dma_start(out, x[:, :, :]).then_inc(stored, 16)
            sp.wait_ge(stored, 16)

        @block.gpsimd
        def _(pool):
            nc.gpsimd.memset(eps_col[:, 0:1], NORM_EPS).then_inc(eps_ready, 1)
            nc.gpsimd.memset(eps_col[:, 1:2], GN_EPS).then_inc(eps_ready, 1)
            nc.gpsimd.memset(eps_col[:, 2:3], 0.5 * KK_SHIFT * float(np.log(2.0))).then_inc(eps_ready, 1)
            for s, kind in enumerate(stages):
                if kind != "ffn":
                    pool.wait_ge(consts_loaded, 32)
                    MIX[kind]["pool"](pool, s)

        @block.scalar
        def _(act):
            early = slice(0, CONST_COLS["ones"].stop)
            act.dma_start(cst[:, early], constants[:, early]).then_inc(ident_loaded, 16)
            act.dma_start(par[:, :], params).then_inc(params_loaded, 16)
            act.wait_ge(params_loaded, 16)
            act.wait_ge(eps_ready, 3)
            for s, kind in enumerate(stages):
                if kind == "ffn":
                    ffn_all_act(act, s)
                else:
                    MIX[kind]["act"](act, s)
            rstd_of(act, len(stages))

        @block.vector
        def _(dve):
            dve.wait_ge(params_loaded, 16)
            dve.wait_ge(ident_loaded, 16)
            for t in range(2):
                dve.wait_ge(x_loaded[t], 16)
            for s, kind in enumerate(stages):
                if kind == "ffn":
                    ffn_all_dve(dve, s)
                else:
                    dve.wait_ge(consts_loaded, 32)
                    MIX[kind]["dve"](dve, s)
            s = len(stages)
            dve.wait_ge(gain_loaded, 16)
            dve.wait_ge(rstd_ready, 2 * s + 2)
            for t in range(2):
                nc.vector.scalar_tensor_tensor(out=x[:, t, :], in0=x[:, t, :], scalar=rstd[:, t:t + 1],
                                               in1=gain_row, op0=ALU.mult, op1=ALU.mult).then_inc(x_ready, 1)

        @block.tensor
        def _(pe):
            pe.wait_ge(ident_loaded, 16)
            for s, kind in enumerate(stages):
                if kind == "ffn":
                    ffn_all_pe(pe, s)
                else:
                    pe.wait_ge(consts_loaded, 32)
                    MIX[kind]["pe"](pe, s)


def kernel(**inputs):
    import concourse.bacc as bacc
    from concourse.bass_utils import run_bass_kernel_spmd

    arrays, shapes = host_arrays(inputs)
    nc = bacc.Bacc("TRN2", target_bir_lowering=False, num_devices=1)
    aps = [nc.dram_tensor(n, a.shape, mybir.dt.from_np(a.dtype), kind="ExternalInput").ap()
           for n, a in arrays.items()]
    out = nc.dram_tensor("out", (P, 2, D), F32, kind="ExternalOutput").ap()
    build(nc, *aps, out)
    r = run_bass_kernel_spmd(nc, [arrays], core_ids=[0])
    return r.results[0]["out"].transpose(1, 0, 2).reshape(1, T, D)


def host_arrays(inputs):
    a = {k: np.asarray(v) for k, v in inputs.items()}
    gu, dn = weight_units(a)
    low_rank = np.zeros((P, 2, RW), np.float32)
    low_rank[:DECAY_RANK, 0] = a["rwkv_w_up"][0]
    low_rank[DECAY_RANK:DECAY_RANK + ICLR_RANK, 0] = a["rwkv_a_up"][0]
    low_rank[:GATE_RANK, 1] = a["rwkv_g_up"][0]
    arrays = {
        "units_gu": gu, "units_dn": dn,
        "x_in": np.ascontiguousarray(a["x"].reshape(2, P, D).transpose(1, 0, 2)),
        "positions": a["positions"],
        "constants": shape_constants(), "params": parameter_columns(a), "low_rank": low_rank,
        "final_gain": a["final_norm_2"].reshape(1, D),
    }
    return arrays, None
```
